# Optimizing a Trainium2 kernel written in Bass

```python
import jax
import jax.numpy as jnp
from jax import lax
import numpy as np

D_MODEL = 1024
BATCH = 1
SEQ = 512
DEPTH = 1
DEC_BATCH = 8
DEC_SEQ = 8
PAST_LEN = 4096
PAGE_SIZE = 128

RET_HEADS = 4
RET_DK = 128
RET_DV = 128
GLA_HEADS = 4
GLA_DK = 64
GLA_DV = 128
GLA_GATE_RANK = 16
GLA_GATE_NORM = 16.0
CHUNK = 64
ROPE_BASE = 10000.0
N_EXPERTS = 64
TOP_K = 8
N_GROUPS = 8
TOPK_GROUPS = 4
EXPERT_FF = 256
SHARED_FF = 256
ROUTED_SCALE = 2.5
MOE_BLOCK = 128
EPS = 1e-6

RET_QK_W = RET_HEADS * RET_DK
RET_V_W = RET_HEADS * RET_DV
GLA_QK_W = GLA_HEADS * GLA_DK
GLA_V_W = GLA_HEADS * GLA_DV
MIX_W = RET_V_W + GLA_V_W
IN_WIDTHS = (RET_QK_W, RET_QK_W, RET_V_W, RET_V_W,
             GLA_QK_W, GLA_QK_W, GLA_V_W, GLA_V_W, GLA_GATE_RANK)
IN_W = sum(IN_WIDTHS)
IN_SPLITS = tuple(int(s) for s in np.cumsum(IN_WIDTHS)[:-1])

kernel_name = "hybrid_retention_gla_moe_step"

def _rms_norm(x, g):
    xf = x.astype(jnp.float32)
    y = xf * lax.rsqrt(jnp.mean(xf * xf, axis=-1, keepdims=True) + EPS)
    return (y * g.astype(jnp.float32)).astype(x.dtype)

def _head_layer_norm(x, w, b):
    xf = x.astype(jnp.float32)
    mu = jnp.mean(xf, axis=-1, keepdims=True)
    var = jnp.mean(jnp.square(xf - mu), axis=-1, keepdims=True)
    y = (xf - mu) * lax.rsqrt(var + EPS) * w.astype(jnp.float32) + b.astype(jnp.float32)
    return y.astype(x.dtype)

def _rotary(x, pos):
    half = x.shape[-1] // 2
    inv_freq = ROPE_BASE ** (-jnp.arange(half, dtype=jnp.float32) / half)
    ang = pos[:, None] * inv_freq[None, :]
    cos = jnp.cos(ang)[None, :, None, :].astype(x.dtype)
    sin = jnp.sin(ang)[None, :, None, :].astype(x.dtype)
    x1, x2 = x[..., :half], x[..., half:]
    return jnp.concatenate([x1 * cos - x2 * sin, x1 * sin + x2 * cos], axis=-1)

def _to_chunks(a, c):
    b, t = a.shape[:2]
    n = -(-t // c)
    a = jnp.pad(a, [(0, 0), (0, n * c - t)] + [(0, 0)] * (a.ndim - 2))
    a = a.reshape((b, n, c) + a.shape[2:])
    return jnp.moveaxis(a, (1, 2), (0, 3))

def _from_chunks(o, t):
    o = jnp.moveaxis(o, (0, 3), (1, 2))
    b, n, c = o.shape[:3]
    return o.reshape((b, n * c) + o.shape[3:])[:, :t]

def _retention(q, k, v, log_gamma, s0):
    b_, t, h, _ = q.shape
    c = min(CHUNK, t)
    g = jnp.broadcast_to(log_gamma[None, None, :], (b_, t, h))
    qc, kc, vc, gc = (_to_chunks(a, c) for a in (q, k, v, g))
    causal = jnp.tril(jnp.ones((c, c), dtype=bool))

    def step(s, blk):
        qb, kb, vb, gb = blk
        qf, kf, vf = qb.astype(jnp.float32), kb.astype(jnp.float32), vb.astype(jnp.float32)
        b = jnp.cumsum(gb.astype(jnp.float32), axis=-1)
        diff = b[..., :, None] - b[..., None, :]
        dmat = jnp.where(causal, jnp.exp(jnp.where(causal, diff, 0.0)), 0.0)
        scores = jnp.einsum("bhid,bhjd->bhij", qf, kf) * dmat
        o = (jnp.einsum("bhij,bhjv->bhiv", scores, vf)
             + jnp.einsum("bhid,bhdv->bhiv", qf * jnp.exp(b)[..., None], s))
        last = b[..., -1:]
        s_new = (s * jnp.exp(last)[..., None]
                 + jnp.einsum("bhjd,bhjv->bhdv", kf * jnp.exp(last - b)[..., None], vf))
        return s_new, o.astype(v.dtype)

    s_fin, oc = lax.scan(step, s0.astype(jnp.float32), (qc, kc, vc, gc))
    return _from_chunks(oc, t), s_fin

def _gla(q, k, v, log_a, s0):
    t = q.shape[1]
    c = min(CHUNK, t)
    qc, kc, vc, gc = (_to_chunks(a, c) for a in (q, k, v, log_a))
    causal = jnp.tril(jnp.ones((c, c), dtype=bool))[:, :, None]

    def step(s, blk):
        qb, kb, vb, gb = blk
        qf, kf, vf = qb.astype(jnp.float32), kb.astype(jnp.float32), vb.astype(jnp.float32)
        b = jnp.cumsum(gb.astype(jnp.float32), axis=2)
        diff = b[:, :, :, None, :] - b[:, :, None, :, :]
        decay = jnp.where(causal, jnp.exp(jnp.where(causal, diff, 0.0)), 0.0)
        scores = jnp.einsum("bhid,bhjd,bhijd->bhij", qf, kf, decay)
        o = (jnp.einsum("bhij,bhjv->bhiv", scores, vf)
             + jnp.einsum("bhid,bhdv->bhiv", qf * jnp.exp(b), s))
        last = b[:, :, -1, :]
        s_new = (s * jnp.exp(last)[..., None]
                 + jnp.einsum("bhjd,bhjv->bhdv", kf * jnp.exp(last[:, :, None, :] - b), vf))
        return s_new, o.astype(v.dtype)

    s_fin, oc = lax.scan(step, s0.astype(jnp.float32), (qc, kc, vc, gc))
    return _from_chunks(oc, t), s_fin

def _mixer(h, pos, s_ret, s_gla, w_in, gla_gate_up, gla_gate_bias,
           ret_norm_w, ret_norm_b, gla_norm_w, w_out):
    b, t, _ = h.shape
    proj = h @ w_in
    rq, rk, rv, rg, gq, gk, gv, gg, ga = jnp.split(proj, IN_SPLITS, axis=-1)
    rq = _rotary(rq.reshape(b, t, RET_HEADS, RET_DK), pos)
    rk = _rotary(rk.reshape(b, t, RET_HEADS, RET_DK), pos) * (RET_DK ** -0.5)
    rv = rv.reshape(b, t, RET_HEADS, RET_DV)
    log_gamma = jnp.log(1.0 - 2.0 ** (-5.0 - jnp.arange(RET_HEADS, dtype=jnp.float32)))
    ro, s_ret_new = _retention(rq, rk, rv, log_gamma, s_ret)
    ro = _head_layer_norm(ro, ret_norm_w, ret_norm_b).reshape(b, t, RET_V_W)
    ro = jax.nn.silu(rg) * ro
    gq = gq.reshape(b, t, GLA_HEADS, GLA_DK) * (GLA_DK ** -0.5)
    gk = gk.reshape(b, t, GLA_HEADS, GLA_DK)
    gv = gv.reshape(b, t, GLA_HEADS, GLA_DV)
    gate_logit = (ga @ gla_gate_up + gla_gate_bias).astype(jnp.float32)
    log_a = (jax.nn.log_sigmoid(gate_logit) / GLA_GATE_NORM).reshape(b, t, GLA_HEADS, GLA_DK)
    go, s_gla_new = _gla(gq, gk, gv, log_a, s_gla)
    go = _rms_norm(go, gla_norm_w).reshape(b, t, GLA_V_W)
    go = jax.nn.silu(gg) * go
    out = jnp.concatenate([ro, go], axis=-1) @ w_out
    return out, s_ret_new, s_gla_new

def _swiglu(x, wg, wu, wd):
    return (jax.nn.silu(x @ wg) * (x @ wu)) @ wd

def _routed_experts(xf, idx, wts, w_gate, w_up, w_down):
    n, d = xf.shape
    m = n * TOP_K
    flat_e = idx.reshape(m)
    flat_tok = jnp.repeat(jnp.arange(n, dtype=jnp.int32), TOP_K)
    flat_w = wts.reshape(m)
    order = jnp.argsort(flat_e)
    se = flat_e[order]
    counts = jnp.bincount(flat_e, length=N_EXPERTS)
    start = jnp.cumsum(counts) - counts
    pcounts = (counts + MOE_BLOCK - 1) // MOE_BLOCK * MOE_BLOCK
    pend = jnp.cumsum(pcounts)
    pstart = pend - pcounts
    dest = pstart[se] + (jnp.arange(m, dtype=jnp.int32) - start[se])
    n_blocks = (m + N_EXPERTS * (MOE_BLOCK - 1) + MOE_BLOCK - 1) // MOE_BLOCK
    p = n_blocks * MOE_BLOCK
    buf_tok = jnp.full((p,), n, jnp.int32).at[dest].set(flat_tok[order])
    buf_w = jnp.zeros((p,), flat_w.dtype).at[dest].set(flat_w[order])
    block_start = jnp.arange(n_blocks, dtype=jnp.int32) * MOE_BLOCK
    block_e = jnp.minimum(jnp.sum(pend[None, :] <= block_start[:, None], axis=1), N_EXPERTS - 1)
    x_pad = jnp.concatenate([xf, jnp.zeros((1, d), xf.dtype)], axis=0)
    xb = x_pad[buf_tok].reshape(n_blocks, MOE_BLOCK, d)

    def run_block(args):
        xblk, e = args
        return _swiglu(xblk, w_gate[e], w_up[e], w_down[e])

    yb = lax.map(run_block, (xb, block_e)).reshape(p, d)
    yb = yb * buf_w[:, None].astype(yb.dtype)
    return jax.ops.segment_sum(yb, buf_tok, num_segments=n + 1)[:n]

def _moe(h, w_router, router_bias, w_exp_gate, w_exp_up, w_exp_down,
         w_sh_gate, w_sh_up, w_sh_down):
    b, t, d = h.shape
    xf = h.reshape(b * t, d)
    n = xf.shape[0]
    scores = jax.nn.sigmoid((xf @ w_router).astype(jnp.float32))
    sel = scores + router_bias.astype(jnp.float32)
    grp = sel.reshape(n, N_GROUPS, N_EXPERTS // N_GROUPS)
    grp_score = jnp.sum(lax.top_k(grp, 2)[0], axis=-1)
    _, top_g = lax.top_k(grp_score, TOPK_GROUPS)
    gmask = jnp.any(top_g[:, :, None] == jnp.arange(N_GROUPS)[None, None, :], axis=1)
    emask = jnp.repeat(gmask, N_EXPERTS // N_GROUPS, axis=1)
    _, idx = lax.top_k(jnp.where(emask, sel, -jnp.inf), TOP_K)
    w = jnp.take_along_axis(scores, idx, axis=-1)
    w = w / jnp.sum(w, axis=-1, keepdims=True) * ROUTED_SCALE
    routed = _routed_experts(xf, idx, w, w_exp_gate, w_exp_up, w_exp_down)
    shared = _swiglu(xf, w_sh_gate, w_sh_up, w_sh_down)
    return (routed + shared).reshape(b, t, d)

def _layer(x, c, pos, s_ret, s_gla, w_ada, b_ada, norm_pre_mix, norm_post_mix,
           norm_pre_ffn, norm_post_ffn, w_in, gla_gate_up, gla_gate_bias,
           ret_norm_w, ret_norm_b, gla_norm_w, w_out, w_router, router_bias,
           w_exp_gate, w_exp_up, w_exp_down, w_sh_gate, w_sh_up, w_sh_down):
    mod = jax.nn.silu(c) @ w_ada + b_ada
    sh1, sc1, g1, sh2, sc2, g2 = (m[:, None, :] for m in jnp.split(mod, 6, axis=-1))
    h = _rms_norm(x, norm_pre_mix) * (1.0 + sc1) + sh1
    mix, s_ret_new, s_gla_new = _mixer(h, pos, s_ret, s_gla, w_in, gla_gate_up, gla_gate_bias,
                                       ret_norm_w, ret_norm_b, gla_norm_w, w_out)
    x = x + g1 * _rms_norm(mix, norm_post_mix)
    h = _rms_norm(x, norm_pre_ffn) * (1.0 + sc2) + sh2
    f = _moe(h, w_router, router_bias, w_exp_gate, w_exp_up, w_exp_down,
             w_sh_gate, w_sh_up, w_sh_down)
    x = x + g2 * _rms_norm(f, norm_post_ffn)
    return x, s_ret_new, s_gla_new

def setup_inputs(seed: int = 0) -> dict:
    key = jax.random.key(seed)
    ks = jax.random.split(key, 32)
    f32 = jnp.float32

    def nrm(k, shape, scale):
        return jax.random.normal(k, shape, f32) * scale

    L = DEPTH
    D = D_MODEL
    return {
        "x_prompt": nrm(ks[0], (BATCH, SEQ, D), 1.0),
        "x_sample": nrm(ks[1], (DEC_BATCH, DEC_SEQ, D), 1.0),
        "state_ret": nrm(ks[2], (L, DEC_BATCH, RET_HEADS, RET_DK, RET_DV), 0.5),
        "state_gla": nrm(ks[3], (L, DEC_BATCH, GLA_HEADS, GLA_DK, GLA_DV), 1.0),
        "c_prompt": nrm(ks[4], (BATCH, D), 1.0),
        "c_sample": nrm(ks[5], (DEC_BATCH, D), 1.0),
        "w_ada": nrm(ks[6], (L, D, 6 * D), 0.2 * D ** -0.5),
        "b_ada": nrm(ks[7], (L, 6 * D), 0.02),
        "norm_pre_mix": 1.0 + nrm(ks[8], (L, D), 0.05),
        "norm_post_mix": 1.0 + nrm(ks[9], (L, D), 0.05),
        "norm_pre_ffn": 1.0 + nrm(ks[10], (L, D), 0.05),
        "norm_post_ffn": 1.0 + nrm(ks[11], (L, D), 0.05),
        "w_in": nrm(ks[12], (L, D, IN_W), D ** -0.5),
        "gla_gate_up": nrm(ks[13], (L, GLA_GATE_RANK, GLA_QK_W), GLA_GATE_RANK ** -0.5),
        "gla_gate_bias": nrm(ks[14], (L, GLA_QK_W), 0.1),
        "ret_norm_w": 1.0 + nrm(ks[15], (L, RET_HEADS, RET_DV), 0.05),
        "ret_norm_b": nrm(ks[16], (L, RET_HEADS, RET_DV), 0.02),
        "gla_norm_w": 1.0 + nrm(ks[17], (L, GLA_HEADS, GLA_DV), 0.05),
        "w_out": nrm(ks[18], (L, MIX_W, D), MIX_W ** -0.5),
        "w_router": nrm(ks[19], (L, D, N_EXPERTS), D ** -0.5),
        "router_bias": nrm(ks[20], (L, N_EXPERTS), 0.01),
        "w_exp_gate": nrm(ks[21], (L, N_EXPERTS, D, EXPERT_FF), D ** -0.5),
        "w_exp_up": nrm(ks[22], (L, N_EXPERTS, D, EXPERT_FF), D ** -0.5),
        "w_exp_down": nrm(ks[23], (L, N_EXPERTS, EXPERT_FF, D), EXPERT_FF ** -0.5),
        "w_sh_gate": nrm(ks[24], (L, D, SHARED_FF), D ** -0.5),
        "w_sh_up": nrm(ks[25], (L, D, SHARED_FF), D ** -0.5),
        "w_sh_down": nrm(ks[26], (L, SHARED_FF, D), SHARED_FF ** -0.5),
    }

def reference(x_prompt, x_sample, state_ret, state_gla, c_prompt, c_sample,
              w_ada, b_ada, norm_pre_mix, norm_post_mix, norm_pre_ffn, norm_post_ffn,
              w_in, gla_gate_up, gla_gate_bias, ret_norm_w, ret_norm_b, gla_norm_w, w_out,
              w_router, router_bias, w_exp_gate, w_exp_up, w_exp_down,
              w_sh_gate, w_sh_up, w_sh_down):
    bp, tp = x_prompt.shape[:2]
    ts = x_sample.shape[1]
    pos_p = jnp.arange(tp, dtype=jnp.float32)
    pos_s = PAST_LEN + jnp.arange(ts, dtype=jnp.float32)
    xp, xs = x_prompt, x_sample
    ret_p, gla_p, ret_s, gla_s = [], [], [], []
    for l in range(DEPTH):
        params = (w_ada[l], b_ada[l], norm_pre_mix[l], norm_post_mix[l], norm_pre_ffn[l],
                  norm_post_ffn[l], w_in[l], gla_gate_up[l], gla_gate_bias[l], ret_norm_w[l],
                  ret_norm_b[l], gla_norm_w[l], w_out[l], w_router[l], router_bias[l],
                  w_exp_gate[l], w_exp_up[l], w_exp_down[l], w_sh_gate[l], w_sh_up[l],
                  w_sh_down[l])
        zr = jnp.zeros((bp, RET_HEADS, RET_DK, RET_DV), jnp.float32)
        zg = jnp.zeros((bp, GLA_HEADS, GLA_DK, GLA_DV), jnp.float32)
        xp, rp, gp = _layer(xp, c_prompt, pos_p, zr, zg, *params)
        xs, rs, gs = _layer(xs, c_sample, pos_s, state_ret[l], state_gla[l], *params)
        ret_p.append(rp.astype(state_ret.dtype))
        gla_p.append(gp.astype(state_gla.dtype))
        ret_s.append(rs.astype(state_ret.dtype))
        gla_s.append(gs.astype(state_gla.dtype))
    return (xp, xs, jnp.stack(ret_p), jnp.stack(gla_p), jnp.stack(ret_s), jnp.stack(gla_s))


_drawn_inputs = setup_inputs


def setup_inputs(seed=0):
    import zlib

    import numpy as np

    out = dict(_drawn_inputs(seed))
    spreads = {}
    factors = {'norm_post_mix': 6.328,
     'norm_pre_ffn': 2.808,
     'norm_post_ffn': 8.0,
     'ret_norm_w': 6.888,
     'ret_norm_b': 8.0,
     'gla_norm_w': 5.802}
    for name, (base, spread) in spreads.items():
        noise = np.random.default_rng([zlib.crc32(name.encode()), seed]).standard_normal(out[name].shape)
        drawn = base * np.exp(spread * noise) if base else spread * noise
        out[name] = jnp.asarray(drawn.astype(out[name].dtype))
    for name, factor in factors.items():
        out[name] = (out[name] * factor).astype(out[name].dtype)
    return out
```

```python
import concourse.bass as bass
from concourse import mybir
from concourse.alu_op_type import AluOpType as ALU
from contextlib import ExitStack
import numpy as np

F32 = mybir.dt.float32
I32 = mybir.dt.int32
U32 = mybir.dt.uint32
ACT = mybir.ActivationFunctionType
AX = mybir.AxisListType

P = 128
D = 1024
KT = D // P
SEQ, SB, SS = 512, 8, 8
NS = SB * SS
N = SEQ + NS
PT = SEQ // P
NT = PT + 1
ROWS = [P] * PT + [NS]
H, DK, GK, DV, RANK = 4, 128, 64, 128, 16
HP = H // 2
CH = 64
NCH = SEQ // CH
RET_W, GK_W = H * DK, H * GK
C_RQ, C_RK, C_RV, C_RG = 0, RET_W, 2 * RET_W, 3 * RET_W
C_GQ = 4 * RET_W
C_GK = C_GQ + GK_W
C_GV = C_GK + GK_W
C_GG = C_GV + RET_W
C_GA = C_GG + RET_W
IN_W = C_GA + RANK
C_GO = C_GQ
E, G, TOPK, TOPG, FF = 64, 8, 8, 4, 256
FK = FF // P
EPS = 1e-6
SCALE = 2.5
PAST = 4096
NCOND = 1 + SB
GAMMA = [1.0 - 2.0 ** (-5.0 - h) for h in range(H)]
EMPTY = 8192.0
FAR = 1.0e6
T = 104
MAXC = -(-N // T)
MAX_BLOCKS = E + N * TOPK // T
MIN_BLOCKS = -(-N * TOPK // T)
ECOL = E + 1
U = 4
RING = 2
AHEAD = 4
GATHER_AHEAD = 3

_consts = {}
_width = 0


def _col(name, n):
    global _width
    _consts[name] = (_width, n)
    _width += n


for _n, _w in [("ident", P), ("ones", P), ("before", P), ("maskg", P), ("gmid", P), ("gcum", P), ("gend", P),
               ("gmid_s", NS), ("gcum_s", NS), ("gend_s", NS), ("maskg_s", NS), ("chunk", 2), ("chunk_s", SB),
               ("dret", H * SEQ), ("dret_s", H * NS), ("cos", NT * 64), ("sin", NT * 64), ("kpow", NT * H),
               ("qpow_s", H * NS), ("seq_cols", SB * NS), ("seq_rows", SB), ("selp", P), ("sels", NS),
               ("upto", E), ("count", P), ("tok", NT), ("tok8", NT)]:
    _col(_n, _w)
CONST_W = _width

MOD0 = CONST_W
PROJ0 = MOD0 + 6 * D
WORK0 = PROJ0 + NT * IN_W
HT0 = WORK0 + 10752
ST0 = HT0 + KT * N
ARENA_W = ST0 + 6 * D
RING_AT = [WORK0, ST0]
W_COLS = (2 * KT * FF, FK * D)


def _constants():
    a = np.zeros((P, CONST_W), np.float32)

    def put(name, v):
        v = np.asarray(v, np.float32)
        v = v.reshape(v.shape[0], -1)
        o, n = _consts[name]
        assert v.shape[1] == n, (name, v.shape, n)
        a[:v.shape[0], o:o + n] = v

    i = np.arange(P)
    put("ident", np.eye(P))
    put("ones", np.ones((P, P)))
    put("before", i[:, None] < i[None, :])

    def gates(size, chunk, suffix):
        j, t = np.arange(size)[:, None], np.arange(size)[None, :]
        same = j // chunk == t // chunk
        mid = t // chunk * chunk + chunk // 2 - 1
        cum = same & (j <= t)
        put("gcum" + suffix, cum / 16.0)
        put("gmid" + suffix, (cum.astype(float) - (same & (j <= mid))) / 16.0)
        put("gend" + suffix, (same & (j > t)) / 16.0)
        put("maskg" + suffix, cum)
        put("chunk" + suffix, (j // chunk == np.arange(size // chunk)[None, :]) / 16.0)

    gates(P, CH, "")
    gates(NS, SS, "_s")
    j, t = np.arange(P)[:, None], np.arange(SEQ)[None, :]
    scale = DK ** -0.5
    put("dret", np.stack([np.where(t >= j, np.float64(g) ** np.maximum(t - j, 0), 0) * scale for g in GAMMA], 1))
    j, t = np.arange(NS)[:, None], np.arange(NS)[None, :]
    put("dret_s", np.stack([np.where((t >= j) & (t // SS == j // SS), np.float64(g) ** np.maximum(t - j, 0), 0) * scale
                            for g in GAMMA], 1))
    half = DK // 2
    inv = (np.float32(10000.0) ** (-np.arange(half, dtype=np.float32) / np.float32(half))).astype(np.float32)
    pos = np.concatenate([np.arange(SEQ), np.tile(PAST + np.arange(SS), SB), np.zeros(P - NS)]).astype(np.float32)
    ang = (pos[:, None] * inv[None, :]).astype(np.float32).reshape(NT, P, half).transpose(1, 0, 2)
    put("cos", np.cos(ang.astype(np.float64)))
    put("sin", np.sin(ang.astype(np.float64)))
    kp = np.zeros((P, NT, H))
    qp = np.zeros((P, H, NS))
    for h, g in enumerate(GAMMA):
        for n in range(PT):
            kp[:, n, h] = np.float64(g) ** (SEQ - 1 - (n * P + i)) * scale
        kp[:NS, PT, h] = np.float64(g) ** (SS - 1 - np.arange(NS) % SS) * scale
        qp[:, h, :] = np.float64(g) ** (np.arange(NS) % SS + 1)
    put("kpow", kp)
    put("qpow_s", qp)
    put("seq_cols", np.broadcast_to(np.arange(NS)[None, None, :] // SS == np.arange(SB)[None, :, None], (P, SB, NS)))
    put("seq_rows", np.arange(NS)[:, None] // SS == np.arange(SB)[None, :])
    put("selp", np.eye(NCOND)[:, [0] * P])
    put("sels", (np.arange(NCOND)[:, None] == 1 + np.arange(NS)[None, :] // SS))
    put("upto", np.arange(E)[:, None] <= np.arange(E)[None, :])
    put("count", np.broadcast_to(i[None, :], (P, P)))
    tok = np.arange(NT)[None, :] * P + i[:, None]
    put("tok", tok - EMPTY)
    put("tok8", tok * TOPK - 1 - EMPTY)
    return a


def hybrid_step(nc, x_prompt, x_sample, state_ret, state_gla, c_prompt, c_sample, w_ada, b_ada, norm_pre_mix,
                norm_post_mix, norm_pre_ffn, norm_post_ffn, w_in, gla_gate_up, gla_gate_bias, ret_norm_w,
                ret_norm_b, gla_norm_w, w_out, w_router, router_bias, w_exp_gate, w_exp_up, w_exp_down, w_sh_gate,
                w_sh_up, w_sh_down, consts, y_prompt, y_sample, ret_p, gla_p, ret_s, gla_s, h2_rows, expert_rows):
    ctx = ExitStack()
    with ctx:
        def sb(name, shape, dt=F32):
            return ctx.enter_context(nc.sbuf_tensor(name, shape, dt))

        def sem(name):
            return ctx.enter_context(nc.semaphore(name))

        arena = sb("arena", [P, ARENA_W])

        def region(at, *dims, rows=P, start=0):
            n = int(np.prod(dims))
            v = arena[start:start + rows, at:at + n]
            if len(dims) == 2:
                return v.rearrange("p (a b) -> p a b", a=dims[0])
            if len(dims) == 3:
                return v.rearrange("p (a b c) -> p a b c", a=dims[0], b=dims[1])
            if len(dims) == 4:
                return v.rearrange("p (a b c d) -> p a b c d", a=dims[0], b=dims[1], c=dims[2])
            return v

        def K(name, rows=P):
            o, n = _consts[name]
            return arena[0:rows, o:o + n]

        ident = K("ident")
        mod = region(MOD0, 6 * D)
        proj = region(PROJ0, NT, IN_W)
        hT = region(HT0, KT, N)
        cond = region(PROJ0, D, rows=NCOND)
        ada_bias = region(PROJ0 + D, 6 * D, rows=NCOND)
        norm_rows = region(PROJ0 + 7 * D, 4, D, rows=NCOND)
        w_ada_buf = region(WORK0, 2, KT, 512)
        condT = sb("condT", [P, KT, NCOND])
        bc1 = region(ST0, 4, D)
        x_buf = region(WORK0 + 8192, 2, D)
        h_buf = region(PROJ0 + 11 * D, 2, D)
        GW = IN_W // 8
        w_in_buf = region(WORK0, 2, KT, GW)
        ss = sb("ss", [P, 4, NT])
        rstd = sb("rstd", [P, 4, NT])
        minus_half = sb("minus_half", [P, 16])
        square_junk = region(PROJ0 + 13 * D, D)
        sq_junk2 = region(PROJ0 + 6 * D, D)
        bc2_tmp = region(PROJ0 + 5 * D, D)
        s0_ret = region(ST0, SB, H, DV)
        s0_gla = region(ST0 + SB * H * DV, SB, HP, DV)
        gate_up = sb("gate_up", [RANK, GK_W])
        gate_bias = sb("gate_bias", [P, GK_W])
        head_w = region(HT0, 3, RET_W)
        head_mu = sb("head_mu", [P, H])
        head_ss = sb("head_ss", [P, NT, 2 * H])
        head_rs = sb("head_rs", [P, NT, 2 * H])
        rot = region(WORK0, 4, 2 * H * 64)
        qkT = region(HT0, 2 * H, N)
        pr = region(WORK0 + 2048, 2, 1280)
        PR_OFF = [0, 512, 896, 1152]
        pr_s = region(WORK0 + 4608, NS, rows=NS)
        qm_r = region(WORK0 + 4672, SB, NS)
        qg_r = region(WORK0 + 5184, NS)
        v_by_seq = region(WORK0 + 5248, SB, DV, rows=NS)
        ret_out = region(WORK0 + 6272, H, DV)
        gated = region(WORK0, NT, 2, GK_W)
        glT = region(WORK0 + 2560, 3, HP, P)
        p_gla = region(WORK0 + 3328, H, P)
        s_gla = region(WORK0 + 3840, NCH + 1, HP, DV)
        z_buf = region(WORK0 + 6144, GK_W)
        ls_buf = region(WORK0 + 6400, GK_W)
        ex = region(WORK0 + 6656, 4, GK_W)
        qm_g = region(WORK0 + 7680, HP, SB, NS)
        v_by_seq_g = region(WORK0 + 8704, SB, DV, rows=NS)
        gaT = region(WORK0 + 9728, P, rows=RANK)
        dec = region(WORK0 + 9856, HP, NCH)
        dec_s = region(WORK0 + 9872, HP, SB)
        w_out_buf = region(WORK0, KT, D)
        bc2 = region(ST0, 6, D)
        x1 = region(PROJ0, NT, D)
        shared = region(PROJ0 + 5 * D, NT, D)
        bcg2 = region(PROJ0 + 10 * D, 2, D)
        pos_tab = region(PROJ0 + 12 * D, MAXC * ECOL * NT)
        info_tab = region(PROJ0 + 12 * D + MAXC * ECOL * NT, ECOL * NT * 3)
        HB0 = PROJ0 + 12 * D + MAXC * ECOL * NT + ECOL * NT * 3
        h2_buf = region(HB0, 2, D)
        w_sh = region(MOD0, KT, 2 * FF)
        w_sh_down_buf = region(MOD0 + KT * 2 * FF, FK, D)
        assert HB0 + 2304 <= WORK0
        w_router_buf = sb("w_router_buf", [P, KT, E])
        r_bias = sb("r_bias", [P, E])
        small_at = [_consts["dret"][0]]

        def small(*dims, rows=P):
            at = small_at[0]
            small_at[0] += int(np.prod(dims))
            assert small_at[0] <= _consts["dret"][0] + H * SEQ
            return region(at, *dims, rows=rows)

        scores, sel, sel2, zeros = small(E), small(E), small(E), small(E)
        top8 = small(G, 8)
        gsc, gsc2 = small(TOPG + G), small(TOPG + G)
        m8 = small(8)
        taken, taken_far = small(NT, E), small(NT, E)
        wsum = small(4)
        blocks_e = small(4, rows=E)
        in_reach = small(P, rows=E)
        rowf = small(5, P, rows=1)
        tab = region(_consts["before"][0] + P, 4, P, rows=1).bitcast(I32)
        onehot = region(HB0, 2, NT, T)
        act_rows = region(HB0 + 1280, 2, FF)
        actT = region(HB0 + 1792, 2, FK, T)
        silu_g = region(WORK0 + 10240, 2, FF)
        w_gu = [region(a, 2, KT, FF) for a in RING_AT]
        w_dn = [region(a + W_COLS[0], FK, D) for a in RING_AT]
        x_rows = region(WORK0 + 6144, 2, D)
        xT = region(WORK0 + 8192, 2, KT, T)
        y_rows = region(HT0, 2, D)
        sh_act = region(WORK0 + 6144, NT, FF)
        sh_silu = region(WORK0 + 6144 + NT * FF, 2, FF)
        sh_actT = region(WORK0 + 6144 + (NT + 2) * FF, NT, FK, P)
        info = sb("info", [P, 2, NT * 3])
        slot_info_kept = sb("slot_info_kept", [P, 3 * (MAX_BLOCKS + U)])
        token_idx = sb("token_idx", [P, U], I32)
        row_idx = sb("row_idx", [P, U], I32)
        slot_w = sb("slot_w", [P, U])
        y_buf = [region(WORK0, TOPK, D), region(HT0, TOPK, D)]
        out_buf = region(MOD0, 2, D)
        sq2 = region(MOD0 + 2 * D, D)
        ps = ctx.enter_context(nc.psum_tensor("ps", [P, 8, 512], F32))

        s_const = sem("consts_in")
        s_cond = sem("cond_in")
        s_rows = sem("rows_in")
        s_small = sem("small_in")
        s_wada = [sem("w_ada_in0"), sem("w_ada_in1")]
        s_silu = sem("cond_silu")
        s_cT = sem("condT_psum")
        s_cTs = sem("condT_ready")
        s_mod = sem("mod_psum")
        s_mod_ev = sem("mod_rows_ready")
        s_fold = sem("mod_folded")
        s_bc = sem("bc_psum")
        s_bc_ev = sem("bc_ready")
        s_x = [sem("x_in0"), sem("x_in1")]
        s_ss = sem("square_sum")
        s_rs = sem("rstd_ready")
        s_h = sem("h_ready")
        s_tr = sem("h_transposed")
        s_hT = sem("hT_ready")
        s_win = [sem("w_in_in0"), sem("w_in_in1")]
        s_pj = sem("proj_psum")
        s_pj_ev = sem("proj_ready")
        s_st = sem("states_in")
        s_v = sem("vector_step")
        s_a = sem("scalar_step")
        s_g = sem("gpsimd_step")
        s_rot = sem("rotated")
        s_rtr = sem("qk_transposed")
        s_qkT = sem("qkT_ready")
        s_ks = sem("k_scaled")
        s_sc = sem("ret_scores")
        s_p = sem("ret_probs")
        s_ro = sem("ret_out_psum")
        s_roe = sem("ret_out_ready")
        s_rsc = sem("ret_s_scores")
        s_rp = sem("ret_s_probs")
        s_rso = sem("ret_s_out")
        s_rsoe = sem("ret_s_out_ready")
        s_vs = sem("v_by_seq_ready")
        s_rkv = sem("ret_kv")
        s_rkve = sem("ret_kv_added")
        s_rst = sem("ret_state_psum")
        s_rste = sem("ret_state_ready")
        s_gat = sem("gaT_psum")
        s_gate = sem("gaT_ready")
        s_z = sem("gate_psum")
        s_ze = sem("gate_logits")
        s_l = sem("softplus")
        s_ls = sem("log_gates")
        s_gx = sem("decay_psum")
        s_gxe = sem("decays")
        s_gm = sem("gated_qk")
        s_gt = sem("gla_transposed")
        s_gte = sem("glaT_ready")
        s_gs = sem("gla_scores")
        s_gp = sem("gla_probs")
        s_kv = sem("gla_kv")
        s_sg = sem("gla_state")
        s_go = sem("gla_out_psum")
        s_goe = sem("gla_out_ready")
        s_qm = sem("gla_q_by_seq")
        s_gvs = sem("gla_v_by_seq")
        s_gkv = sem("gla_s_kv")
        s_gkve = sem("gla_s_kv_added")
        s_nq = sem("head_squares")
        s_nv = sem("head_vars")
        s_nr = sem("head_rstd")
        s_ng = sem("gates_silu")
        s_nd = sem("heads_done")
        s_mt = sem("mix_transposed")
        s_mte = sem("mixT_ready")
        s_wout = sem("w_out_in")
        s_wo = sem("mix_psum")
        s_q1 = sem("mix_square_sum")
        s_r1 = sem("mix_rstd")
        s_x1 = sem("x1_ready")
        s_q2 = sem("x1_square_sum")
        s_r2 = sem("x1_rstd")
        s_h2 = sem("h2_ready")
        s_h2d = [sem("h2_stored0"), sem("h2_stored1")]
        s_h2t = sem("h2_transposed")
        s_h2T = sem("h2T_ready")
        s_xr = [sem("x_again0"), sem("x_again1")]
        s_lg = sem("logits")
        s_sig = sem("router_scores")
        s_tk = sem("experts_taken")
        s_pos = sem("positions")
        s_pend = sem("block_ends")
        s_blk = sem("block_counts")
        s_rch = sem("blocks_in_reach")
        s_trow = sem("table_psum")
        s_tab = sem("table_ready")
        s_wsh = sem("w_shared_in")
        s_sgu = sem("shared_gate_up")
        s_ssi = sem("shared_silu")
        s_sm = sem("shared_act")
        s_sht = sem("shared_actT_psum")
        s_shte = sem("shared_actT")
        s_sy = sem("shared_psum")
        s_sye = sem("shared_ready")
        s_wgu = [sem(f"w_gate_up_in{b}") for b in range(U)]
        s_wdn = [sem(f"w_down_in{b}") for b in range(U)]
        s_oh = sem("onehot_ready")
        s_info = sem("slot_info_psum")
        s_kept = sem("slot_info_kept_ready")
        s_idx = sem("gather_index_ready")
        s_xg = [sem("x_rows_in0"), sem("x_rows_in1")]
        s_xt = sem("xT_psum")
        s_xta = sem("xT_low_ready")
        s_xtv = sem("xT_high_ready")
        s_gu = sem("gate_up_psum")
        s_si = sem("silu_ready")
        s_act = sem("act_ready")
        s_at = sem("actT_psum")
        s_ate = sem("actT_ready")
        s_y = sem("y_psum")
        s_ya = sem("y_low_ready")
        s_yv = sem("y_high_ready")
        s_ys = [sem(f"y_rows_out{b}") for b in range(U)]
        s_tick = sem("rows_scattered")
        s_free = sem("y_rows_free")
        s_wt = sem("slot_weight_and_row_ready")
        s_pulse = sem("gpsimd_pulse")
        s_sq = sem("head_squares_ready")
        s_rowtile = sem("row_tile_changed")
        s_hw = sem("head_weights_in")
        s_yb = [sem("y_again0"), sem("y_again1")]
        s_add = sem("combined")
        s_q3 = sem("ffn_square_sum")
        s_r3 = sem("ffn_rstd")
        s_fin = sem("out_ready")
        s_out = sem("outputs_stored")

        GS_BANK, GO_BANK = (5, 0), (7, 1)
        block = ctx.enter_context(nc.Block())

        def tok_rows(a_prompt, a_sample, t):
            return a_prompt[0, t * P:(t + 1) * P, :] if t < PT else a_sample.rearrange("b s d -> (b s) d")

        def last_turn(eng):
            return eng.value_load(tab[0:1, 3, 0:1], min_val=-(-MIN_BLOCKS // U) - 1, max_val=-(-MAX_BLOCKS // U) - 1)

        @block.sync
        def _(sp):
            sp.dma_start(cond[0:1, :], c_prompt[:, :]).then_inc(s_cond, 16)
            sp.dma_start(cond[1:NCOND, :], c_sample[:, :]).then_inc(s_cond, 16)
            sp.dma_start(arena[:, 0:CONST_W], consts).then_inc(s_const, 16)
            ada = w_ada[0].rearrange("(k p) n -> p k n", p=P)
            for b in range(2):
                sp.dma_start(w_ada_buf[:, b], ada[:, :, b * 512:(b + 1) * 512]).then_inc(s_wada[b], 16)
            sp.dma_start(ada_bias, b_ada[0:1, :].broadcast_to([NCOND, 6 * D])).then_inc(s_rows, 16)
            for n, w in enumerate((norm_pre_mix, norm_post_mix, norm_pre_ffn, norm_post_ffn)):
                sp.dma_start(norm_rows[:, n], w[0:1, :].broadcast_to([NCOND, D])).then_inc(s_rows, 16)
            with sp.Fori(1, 6) as i:
                for b in range(2):
                    sp.wait_ge(s_mod, 2 * i + b - 1)
                    sp.dma_start(w_ada_buf[:, b], ada[:, :, bass.ds((2 * i + b) * 512, 512)]).then_inc(s_wada[b], 16)
            for t in range(2):
                sp.dma_start(x_buf[0:ROWS[t], t % 2], tok_rows(x_prompt, x_sample, t)).then_inc(s_x[t % 2], 16)
            sp.dma_start(gate_up[:, :], gla_gate_up[0]).then_inc(s_small, 16)
            sp.dma_start(gate_bias[:, :], gla_gate_bias[0:1, :].broadcast_to([P, GK_W])).then_inc(s_small, 16)
            sp.dma_start(w_router_buf[:, :, :], w_router[0].rearrange("(p k) e -> p k e", k=KT)).then_inc(s_small, 16)
            sp.dma_start(r_bias[:, :], router_bias[0:1, :].broadcast_to([P, E])).then_inc(s_small, 16)
            sp.wait_ge(s_mod, 12)
            win = w_in[0].rearrange("(k p) n -> p k n", p=P)
            for b in range(2):
                sp.dma_start(w_in_buf[:, b], win[:, :, b * GW:(b + 1) * GW]).then_inc(s_win[b], 16)
            for t in range(2, NT):
                sp.wait_ge(s_h, t - 1)
                sp.dma_start(x_buf[0:ROWS[t], t % 2], tok_rows(x_prompt, x_sample, t)).then_inc(s_x[t % 2], 16)
            sp.wait_ge(s_h, NT)
            sp.dma_start(s0_ret, state_ret[0].rearrange("b h d v -> d b h v")).then_inc(s_st, 16)
            for h in range(H):
                sp.dma_start(s0_gla[(h % 2) * GK:(h % 2 + 1) * GK, :, h // 2, :],
                             state_gla[0, :, h].rearrange("b d v -> d b v")).then_inc(s_st, 16)
            with sp.Fori(1, 4) as i:
                for b in range(2):
                    sp.wait_ge(s_pj, (2 * i + b - 1) * NT)
                    sp.dma_start(w_in_buf[:, b], win[:, :, bass.ds((2 * i + b) * GW, GW)]).then_inc(s_win[b], 16)
            sp.wait_ge(s_rste, 1)
            sp.dma_start(ret_p[0, 0].rearrange("h d v -> d h v"), ret_out).then_inc(s_out, 16)
            sp.wait_ge(s_rkve, 2 * H)
            sp.dma_start(ret_s[0].rearrange("b h d v -> d b h v"), s0_ret).then_inc(s_out, 16)
            sp.wait_ge(s_rso, H)
            sp.wait_ge(s_ro, H)
            for n, w in enumerate((ret_norm_w, ret_norm_b, gla_norm_w)):
                sp.dma_start(head_w[:, n], w.rearrange("a h v -> a (h v)").broadcast_to([P, RET_W])).then_inc(s_hw, 16)
            sp.wait_ge(s_sg, NCH)
            for h in range(H):
                sp.dma_start(gla_p[0, 0, h], s_gla[(h % 2) * GK:(h % 2 + 1) * GK, NCH, h // 2, :]).then_inc(s_out, 16)
            sp.wait_ge(s_gkve, 2 * H)
            for h in range(H):
                sp.dma_start(gla_s[0, :, h].rearrange("b d v -> d b v"),
                             s0_gla[(h % 2) * GK:(h % 2 + 1) * GK, :, h // 2, :]).then_inc(s_out, 16)
            sp.wait_ge(s_goe, NT)
            sp.wait_ge(s_out, 16 * (2 + 2 * H))
            sp.dma_start(w_out_buf, w_out[0].rearrange("(k p) n -> p k n", p=P)).then_inc(s_wout, 16)
            for t in range(NT):
                if t >= 2:
                    sp.wait_ge(s_x1, t - 1)
                sp.dma_start(x_buf[0:ROWS[t], t % 2], tok_rows(x_prompt, x_sample, t)).then_inc(s_xr[t % 2], 16)
                if t == 1:
                    sp.wait_ge(s_bc, 4 + 8)
                    for n, w in enumerate((w_sh_gate, w_sh_up)):
                        sp.dma_start(w_sh[:, :, n * FF:(n + 1) * FF],
                                     w[0].rearrange("(p k) f -> p k f", k=KT)).then_inc(s_wsh, 16)
                    sp.dma_start(w_sh_down_buf, w_sh_down[0].rearrange("(p k) d -> p k d", k=FK)).then_inc(s_wsh, 16)
            for t in range(NT):
                sp.wait_ge(s_h2, t + 1)
                sp.dma_start(h2_rows[t * P:t * P + ROWS[t], :], h2_buf[0:ROWS[t], t % 2]).then_inc(s_h2d[t % 2], 16)

            def load_block(j, b, wait):
                r = b % RING
                e = sp.value_load(tab[0:1, 2, bass.ds(j, 1)] if not isinstance(j, int) else tab[0:1, 2, j:j + 1],
                                  min_val=0, max_val=E - 1)
                if wait:
                    sp.wait_ge(s_gu, j - RING + 1)
                gate = w_exp_gate[0, bass.ds(e, 1)].rearrange("a (p k) f -> (a p) k f", k=KT)
                up = w_exp_up[0, bass.ds(e, 1)].rearrange("a (p k) f -> (a p) k f", k=KT)
                down = w_exp_down[0, bass.ds(e, 1)].rearrange("a (p k) d -> (a p) k d", k=FK)
                sp.dma_start(w_gu[r][:, 0], gate).then_inc(s_wgu[b], 16)
                sp.dma_start(w_gu[r][:, 1], up).then_inc(s_wgu[b], 16)
                if wait:
                    sp.wait_ge(s_y, j - RING + 1)
                sp.dma_start(w_dn[r], down).then_inc(s_wdn[b], 16)

            sp.wait_ge(s_tab, 1)
            sp.wait_ge(s_wo, NT)
            sp.wait_ge(s_h2, NT)
            for j in range(U):
                load_block(j, j, j >= RING)
            last = last_turn(sp)
            with sp.Fori(0, last) as i:
                for b in range(U):
                    load_block(i * U + (U + b), b, True)
            sp.wait_ge(s_y, last * U + U)
            sp.wait_ge(s_tick, 1)
            rows_by_tok = expert_rows.rearrange("(n k) d -> n k d", k=TOPK)
            for t in range(NT):
                if t >= 2:
                    sp.wait_ge(s_add, t - 1)
                sp.dma_start(y_buf[t % 2][0:ROWS[t]], rows_by_tok[t * P:t * P + ROWS[t]]).then_inc(s_yb[t % 2], 16)
                if t >= 1:
                    sp.wait_ge(s_fin, t)
                    sp.dma_start(tok_rows(y_prompt, y_sample, t - 1), out_buf[0:ROWS[t - 1], (t - 1) % 2]).then_inc(s_out, 16)
            sp.wait_ge(s_fin, NT)
            sp.dma_start(tok_rows(y_prompt, y_sample, NT - 1), out_buf[0:ROWS[NT - 1], (NT - 1) % 2]).then_inc(s_out, 16)
            sp.wait_ge(s_out, 16 * (2 + 2 * H + NT))

        @block.gpsimd
        def _(g):
            steps = [0]

            def step(ins):
                steps[0] += 1
                ins.then_inc(s_g, 1)
                g.wait_ge(s_g, steps[0])

            g.sem_inc(s_free, 2)
            step(g.memset(minus_half[:, :], -0.5))

            def inverse_root(out, total, cols, width, ready):
                step(g.tensor_scalar(out, total, 1.0 / width, EPS, ALU.mult, ALU.add))
                g.tensor_tensor(out, out, minus_half[0:out.shape[0], 0:cols], ALU.pow).then_inc(ready, 1)

            for t in range(NT):
                R = ROWS[t]
                g.wait_ge(s_ss, t + 1)
                inverse_root(rstd[0:R, 0, t:t + 1], ss[0:R, 0, t:t + 1], 1, D, s_rs)
            for t in range(NT):
                R = ROWS[t]
                g.wait_ge(s_nv, t + 1)
                inverse_root(head_rs[0:R, t], head_ss[0:R, t], 2 * H, DV, s_nr)
            for t in range(NT):
                R = ROWS[t]
                g.wait_ge(s_q1, t + 1)
                inverse_root(rstd[0:R, 1, t:t + 1], ss[0:R, 1, t:t + 1], 1, D, s_r1)
                g.wait_ge(s_q2, t + 1)
                inverse_root(rstd[0:R, 2, t:t + 1], ss[0:R, 2, t:t + 1], 1, D, s_r2)

            last_gather = g.to_reg(N - 1)
            last_scatter = g.to_reg(N * TOPK - 1)

            def gather(j, b, wait=True):
                g.wait_ge(s_idx, j + 1)
                if wait:
                    g.wait_ge(s_xt, j - 1)
                g.sem_inc(s_pulse, 1)
                g.indirect_dma_start(x_rows[0:T, b % 2], None, h2_rows[:, :],
                                     bass.IndirectOffsetOnAxis(token_idx[0:T, b:b + 1].bitcast(U32), 0),
                                     bounds_check=last_gather, oob_is_err=False).then_inc(s_xg[b % 2], 16)

            def scatter(j, b):
                g.wait_ge(s_ya, j + 2)
                g.wait_ge(s_yv, j + 2)
                g.sem_inc(s_pulse, 1)
                g.indirect_dma_start(expert_rows[:, :], bass.IndirectOffsetOnAxis(row_idx[0:T, b:b + 1].bitcast(U32), 0),
                                     y_rows[0:T, b % 2], None, bounds_check=last_scatter,
                                     oob_is_err=False).then_inc(s_ys[b], 16)

            g.wait_ge(s_sye, NT)
            step(g.memset(x_rows, 0.0))
            g.wait_ge(s_h2, NT)
            g.wait_ge(s_h2d[0], 48)
            g.wait_ge(s_h2d[1], 32)
            g.wait_ge(s_tab, 1)
            for j in range(GATHER_AHEAD):
                gather(j, j, j >= 2)

            def turn(i, is_last):
                for b in range(U):
                    if not is_last or b + GATHER_AHEAD < U:
                        gather(i * U + (b + GATHER_AHEAD), (b + GATHER_AHEAD) % U)
                    scatter(i * U + b, b)
                    g.wait_ge(s_ys[b], 16 * i + 16)
                    g.sem_inc(s_free, 1)

            last = last_turn(g)
            with g.Fori(0, last) as i:
                turn(i, False)
            turn(last, True)
            g.sem_inc(s_tick, 1)
            for t in range(NT):
                R = ROWS[t]
                g.wait_ge(s_q3, t + 1)
                inverse_root(rstd[0:R, 3, t:t + 1], ss[0:R, 3, t:t + 1], 1, D, s_r3)

        @block.scalar
        def _(a):
            steps = [0]

            def step(ins):
                steps[0] += 1
                ins.then_inc(s_a, 1)
                a.wait_ge(s_a, steps[0])

            a.sem_inc(s_pj_ev, NT)
            a.sem_inc(s_ya, 1)
            a.wait_ge(s_cond, 32)
            a.activation(cond, cond, ACT.Silu).then_inc(s_silu, 1)
            for n in range(4):
                a.wait_ge(s_bc, n + 1)
                R = P if n < 2 else NS
                a.activation(bc1[0:R, n].rearrange("p (c n) -> p c n", c=2), ps[0:R, 2 * n:2 * n + 2], ACT.Copy).then_inc(s_bc_ev, 1)
            for t in range(NT):
                R = ROWS[t]
                a.wait_ge(s_x[t % 2], 16 * (t // 2 + 1))
                if t:
                    a.wait_ge(s_ss, t)
                a.activation(square_junk[0:R], x_buf[0:R, t % 2], ACT.Square, accum_out=ss[0:R, 0, t:t + 1]).then_inc(s_ss, 1)
                for half in range(2):
                    a.wait_ge(s_tr, 2 * t + half + 1)
                    a.activation(hT[:, 4 * half:4 * half + 4, t * P:t * P + R],
                                 ps[:, (2 * t + half) % 4].rearrange("p (k r) -> p k r", k=4)[:, :, 0:R],
                                 ACT.Copy).then_inc(s_hT, 1)
            with a.Fori(0, 4) as i:
                for b in range(2):
                    for t in range(NT):
                        a.wait_ge(s_pj, (2 * i + b) * NT + t + 1)
                        a.activation(proj[0:ROWS[t], t, bass.ds((2 * i + b) * GW, GW)], ps[0:ROWS[t], t, 0:GW],
                                     ACT.Copy).then_inc(s_pj_ev, 1)
            for t in range(NT):
                R = ROWS[t]
                for half in range(2):
                    a.wait_ge(s_rtr, 2 * t + half + 1)
                    a.activation(qkT[:, 4 * half:4 * half + 4, t * P:t * P + R],
                                 ps[:, (2 * t + half) % 4].rearrange("p (k r) -> p k r", k=4)[:, :, 0:R],
                                 ACT.Copy).then_inc(s_qkT, 1)
            for h in range(H):
                a.wait_ge(s_ro, h + 1)
                a.activation(proj[:, 0:PT, C_RQ + h * DV:C_RQ + (h + 1) * DV],
                             ps[:, 6 + h % 2].rearrange("p (t v) -> p t v", t=PT), ACT.Copy).then_inc(s_roe, 1)
                a.wait_ge(s_rso, h + 1)
                a.activation(proj[0:NS, PT, C_RQ + h * DV:C_RQ + (h + 1) * DV], ps[0:NS, 2, 0:DV],
                             ACT.Copy).then_inc(s_rsoe, 1)
            a.wait_ge(s_rst, 1)
            a.activation(ret_out, ps[:, 0].rearrange("p (h v) -> p h v", h=H), ACT.Copy).then_inc(s_rste, 1)
            for t in range(NT):
                R = ROWS[t]
                a.wait_ge(s_ze, t + 1)
                if t:
                    a.wait_ge(s_gm, t)
                step(a.activation(ex[0:R, 0], z_buf[0:R], ACT.Abs))
                step(a.activation(ex[0:R, 1], ex[0:R, 0], ACT.Exp, scale=-1.0))
                a.activation(ex[0:R, 2], ex[0:R, 1], ACT.Ln, bias=1.0).then_inc(s_l, 1)
                a.wait_ge(s_gx, t + 1)
                e0 = ps[0:R, 1]
                step(a.activation(ex[0:R, 0], e0[:, 0:GK_W], ACT.Exp))
                step(a.activation(ex[0:R, 1], e0[:, 0:GK_W], ACT.Exp, scale=-1.0))
                step(a.activation(ex[0:R, 2], e0[:, GK_W:2 * GK_W], ACT.Exp))
                step(a.activation(ex[0:R, 3], ps[0:R, 2, 0:GK_W], ACT.Exp))
                if t < PT:
                    a.activation(dec[:, :, 2 * t:2 * t + 2], ps[:, 2, GK_W:GK_W + 2 * HP].rearrange("p (h c) -> p h c", h=HP),
                                 ACT.Exp).then_inc(s_gxe, 1)
                else:
                    a.activation(dec_s, ps[:, 2, GK_W:GK_W + SB * HP].rearrange("p (h c) -> p h c", h=HP),
                                 ACT.Exp).then_inc(s_gxe, 1)
            for t in range(NT):
                R = ROWS[t]
                for n in range(2):
                    cnt = 3 if n == 0 else 3
                    a.wait_ge(s_gt, 2 * t + n + 1)
                    if n == 0 and t:
                        a.wait_ge(s_go, t)
                    a.activation(glT[:, :, n, 0:R], ps[:, 3 + n].rearrange("p (k r) -> p k r", k=4)[:, 0:3, 0:R],
                                 ACT.Copy).then_inc(s_gte, 1)
                a.wait_ge(s_go, t + 1)
                for odd in range(2):
                    o = a.activation(proj[0:R, t, C_GO:C_GO + RET_W].rearrange("p (h v) -> p h v", h=H)[:, odd:H:2],
                                     ps[0:R, GO_BANK[odd]].rearrange("p (h v) -> p h v", h=H)[:, odd:H:2], ACT.Copy)
                    if odd:
                        o.then_inc(s_goe, 1)
                    else:
                        step(o)
            for t in range(NT):
                R = ROWS[t]
                step(a.activation(proj[0:R, t, C_RG:C_RG + RET_W], proj[0:R, t, C_RG:C_RG + RET_W], ACT.Silu))
                a.activation(proj[0:R, t, C_GG:C_GG + RET_W], proj[0:R, t, C_GG:C_GG + RET_W], ACT.Silu).then_inc(s_ng, 1)
            for t in range(NT):
                R = ROWS[t]
                a.wait_ge(s_nq, t + 1)
                step(a.activation(proj[0:R, t, C_RK:C_RK + RET_W], proj[0:R, t, C_RQ:C_RQ + RET_W], ACT.Square))
                a.activation(proj[0:R, t, C_RV:C_RV + RET_W], proj[0:R, t, C_GO:C_GO + RET_W], ACT.Square).then_inc(s_sq, 1)
            for n in range(6):
                a.wait_ge(s_bc, 4 + n + 1)
                R = P if n < 3 else NS
                a.activation(bc2[0:R, n].rearrange("p (c n) -> p c n", c=2), ps[0:R, 4 + 2 * (n % 2):6 + 2 * (n % 2)],
                             ACT.Copy).then_inc(s_bc_ev, 1)
            for t in range(NT):
                R = ROWS[t]
                if t == 0:
                    a.wait_ge(s_nd, NT)
                for half in range(2):
                    a.wait_ge(s_mt, 2 * t + half + 1)
                    a.activation(hT[:, 4 * half:4 * half + 4, t * P:t * P + R],
                                 ps[:, (2 * t + half) % 4].rearrange("p (k r) -> p k r", k=4)[:, :, 0:R],
                                 ACT.Copy).then_inc(s_mte, 1)
            for n in range(2):
                a.wait_ge(s_bc, 4 + 6 + n + 1)
                R = P if n < 1 else NS
                a.activation(bcg2[0:R, n].rearrange("p (c n) -> p c n", c=2), ps[0:R, 4 + 2 * (n % 2):6 + 2 * (n % 2)],
                             ACT.Copy).then_inc(s_bc_ev, 1)
            for t in range(NT):
                R = ROWS[t]
                a.wait_ge(s_wo, t + 1)
                a.activation(sq_junk2[0:R].rearrange("p (c n) -> p c n", c=2), ps[0:R, 2 * (t % 2):2 * (t % 2) + 2],
                             ACT.Square, accum_out=ss[0:R, 1, t:t + 1]).then_inc(s_q1, 1)
                a.wait_ge(s_q1, t + 1)
                a.wait_ge(s_x1, t + 1)
                a.activation(sq_junk2[0:R], x1[0:R, t], ACT.Square, accum_out=ss[0:R, 2, t:t + 1]).then_inc(s_q2, 1)
                a.wait_ge(s_q2, t + 1)
                for half in range(2):
                    a.wait_ge(s_h2t, 2 * t + half + 1)
                    a.activation(hT[:, 4 * half:4 * half + 4, t * P:t * P + R],
                                 ps[:, 4 + (2 * t + half) % 2].rearrange("p (k r) -> p k r", k=4)[:, :, 0:R],
                                 ACT.Copy).then_inc(s_h2T, 1)
            for t in range(NT):
                R = ROWS[t]
                a.wait_ge(s_lg, t + 1)
                if t:
                    a.wait_ge(s_tk, t)
                a.activation(scores[0:R], ps[0:R, 6 + t % 2, 0:E], ACT.Sigmoid).then_inc(s_sig, 1)
            for t in range(NT):
                R = ROWS[t]
                a.wait_ge(s_sgu, t + 1)
                if t >= 2:
                    a.wait_ge(s_sm, t - 1)
                a.activation(sh_silu[0:R, t % 2], ps[0:R, t % 2, 0:FF], ACT.Silu).then_inc(s_ssi, 1)
            for t in range(NT):
                R = ROWS[t]
                a.wait_ge(s_sht, t + 1)
                a.activation(sh_actT[:, t, :, 0:R], ps[:, 2 + t % 2, 0:FK * P].rearrange("p (k r) -> p k r", k=FK)[:, :, 0:R],
                             ACT.Copy).then_inc(s_shte, 1)
            for t in range(NT):
                R = ROWS[t]
                a.wait_ge(s_sy, t + 1)
                a.activation(shared[0:R, t].rearrange("p (c n) -> p c n", c=2), ps[0:R, 4 + 2 * (t % 2):6 + 2 * (t % 2)],
                             ACT.Copy).then_inc(s_sye, 1)

            def silu(j, b):
                a.wait_ge(s_gu, j + 1)
                a.activation(silu_g[0:T, b % 2], ps[0:T, b % 2, 0:FF], ACT.Silu).then_inc(s_si, 1)

            def x_low(j, b):
                a.wait_ge(s_xt, j + 1)
                a.activation(xT[:, b % 2, 0:4, :], ps[:, 4, 0:4 * T].rearrange("p (k r) -> p k r", k=4), ACT.Copy).then_inc(s_xta, 1)

            a.wait_ge(s_tab, 1)
            a.wait_ge(s_sye, NT)
            for j in range(2):
                x_low(j, j)
                if j == 0:
                    silu(0, 0)

            def turn(i, is_last):
                for b in range(U):
                    if not is_last or b + 1 < U:
                        silu(i * U + (b + 1), b + 1)
                    if not is_last or b + 2 < U:
                        x_low(i * U + (b + 2), b + 2)
                    a.wait_ge(s_y, i * U + (b + 1))
                    a.wait_ge(s_wt, i * (2 * U) + (2 * b + 2))
                    a.wait_ge(s_free, i * U + (b + 1))
                    a.activation(y_rows[0:T, b % 2, 0:512], ps[0:T, 2], ACT.Copy, scale=slot_w[0:T, b:b + 1]).then_inc(s_ya, 1)

            last = last_turn(a)
            with a.Fori(0, last) as i:
                turn(i, False)
            turn(last, True)
            for t in range(NT):
                R = ROWS[t]
                a.wait_ge(s_add, t + 1)
                a.activation(sq2[0:R], y_buf[t % 2][0:R, 0], ACT.Square, accum_out=ss[0:R, 3, t:t + 1]).then_inc(s_q3, 1)
                a.wait_ge(s_q3, t + 1)

        @block.vector
        def _(v):
            steps = [0]

            def step(ins):
                steps[0] += 1
                ins.then_inc(s_v, 1)
                v.wait_ge(s_v, steps[0])

            def mark(ins, s, k):
                ins.then_inc(s, 1)
                v.wait_ge(s, k)

            v.sem_inc(s_mod_ev, 2)
            v.sem_inc(s_yv, 1)
            v.wait_ge(s_cT, 1)
            v.tensor_copy(condT[:, :, :], ps[:, 0, 0:KT * NCOND].rearrange("p (k c) -> p k c", k=KT)).then_inc(s_cTs, 1)
            v.wait_ge(s_rows, 16 * 5)
            with v.Fori(0, 6) as i:
                for b in range(2):
                    v.wait_ge(s_mod, 2 * i + b + 1)
                    v.tensor_tensor(mod[0:NCOND, bass.ds((2 * i + b) * 512, 512)], ps[0:NCOND, b],
                                    ada_bias[:, bass.ds((2 * i + b) * 512, 512)], ALU.add).then_inc(s_mod_ev, 1)
            v.wait_ge(s_mod_ev, 2 + 12)
            for at, n, one in ((1, 0, 1.0), (2, 1, 0.0), (4, 2, 1.0), (5, 3, 0.0)):
                m = mod[0:NCOND, at * D:(at + 1) * D]
                mark(v.scalar_tensor_tensor(out=m, in0=m, scalar=one, in1=norm_rows[:, n], op0=ALU.add, op1=ALU.mult),
                     s_fold, {1: 1, 2: 2, 4: 3, 5: 4}[at])
            for t in range(NT):
                R = ROWS[t]
                if t == 0:
                    v.wait_ge(s_bc_ev, 4)
                A, S = (0, 1) if t < PT else (2, 3)
                v.wait_ge(s_x[t % 2], 16 * (t // 2 + 1))
                v.wait_ge(s_rs, t + 1)
                if t >= 2:
                    v.wait_ge(s_tr, 2 * (t - 1))
                step(v.scalar_tensor_tensor(out=h_buf[0:R, t % 2], in0=x_buf[0:R, t % 2], scalar=rstd[0:R, 0, t:t + 1],
                                            in1=bc1[0:R, A], op0=ALU.mult, op1=ALU.mult))
                mark(v.tensor_tensor(h_buf[0:R, t % 2], h_buf[0:R, t % 2], bc1[0:R, S], ALU.add), s_h, t + 1)
            v.wait_ge(s_pj_ev, 9 * NT)
            v.wait_ge(s_small, 16 * 4)
            for t in range(NT):
                R = ROWS[t]
                qk = proj[0:R, t, 0:2 * RET_W].rearrange("p (h c d) -> p h c d", h=2 * H, c=2)
                lo, hi = qk[:, :, 0], qk[:, :, 1]
                c = K("cos", R)[:, t * 64:(t + 1) * 64].unsqueeze(1).broadcast_to([R, 2 * H, 64])
                s = K("sin", R)[:, t * 64:(t + 1) * 64].unsqueeze(1).broadcast_to([R, 2 * H, 64])
                r4 = [rot[0:R, n].rearrange("p (h d) -> p h d", h=2 * H) for n in range(4)]
                for n, (x, f) in enumerate(((lo, c), (hi, s), (lo, s), (hi, c))):
                    step(v.tensor_tensor(r4[n], x, f, ALU.mult))
                step(v.tensor_tensor(lo, r4[0], r4[1], ALU.subtract))
                mark(v.tensor_tensor(hi, r4[2], r4[3], ALU.add), s_rot, t + 1)
            for t in range(NT):
                R = ROWS[t]
                v.wait_ge(s_rtr, 2 * t + 2)
                kk = proj[0:R, t, C_RK:C_RK + RET_W].rearrange("p (h d) -> p h d", h=H)
                kp = K("kpow", R)[:, t * H:(t + 1) * H].unsqueeze(2).broadcast_to([R, H, DK])
                mark(v.tensor_tensor(kk, kk, kp, ALU.mult), s_ks, t + 1)
            v.wait_ge(s_st, 16 * (1 + H))
            for h in range(H):
                for J in range(PT):
                    n = SEQ - J * P
                    v.wait_ge(s_sc, PT * h + J + 1)
                    if J == 0 and h >= 2:
                        v.wait_ge(s_ro, h - 1)
                    mark(v.tensor_tensor(pr[:, h % 2, PR_OFF[J]:PR_OFF[J] + n], ps[:, 4 + J % 2, 0:n],
                                         K("dret")[:, h * SEQ:h * SEQ + n], ALU.mult), s_p, PT * h + J + 1)
                v.wait_ge(s_rsc, h + 1)
                if h:
                    v.wait_ge(s_rso, h)
                    v.wait_ge(s_rkv, 2 * h)
                step(v.tensor_tensor(qg_r, qkT[:, h, SEQ:N], K("qpow_s")[:, h * NS:(h + 1) * NS], ALU.mult))
                step(v.tensor_tensor(qm_r, qg_r.unsqueeze(1).broadcast_to([P, SB, NS]),
                                     K("seq_cols").rearrange("p (b n) -> p b n", b=SB), ALU.mult))
                mark(v.tensor_tensor(pr_s, ps[0:NS, 1, 0:NS], K("dret_s", NS)[:, h * NS:(h + 1) * NS], ALU.mult), s_rp, h + 1)
                mark(v.tensor_tensor(v_by_seq,
                                     proj[0:NS, PT, C_RV + h * DV:C_RV + (h + 1) * DV].unsqueeze(1).broadcast_to([NS, SB, DV]),
                                     K("seq_rows", NS).unsqueeze(2).broadcast_to([NS, SB, DV]), ALU.mult), s_vs, h + 1)
                v.wait_ge(s_rso, h + 1)
                for half in range(2):
                    v.wait_ge(s_rkv, 2 * h + half + 1)
                    st = s0_ret[:, half * 4:half * 4 + 4, h, :]
                    mark(v.scalar_tensor_tensor(out=st, in0=st, scalar=float(np.float32(GAMMA[h] ** SS)),
                                                in1=ps[:, 3].rearrange("p (b v) -> p b v", b=4),
                                                op0=ALU.mult, op1=ALU.add), s_rkve, 2 * h + half + 1)
            v.wait_ge(s_rste, 1)
            v.wait_ge(s_out, 32)
            for t in range(NT):
                R = ROWS[t]
                v.wait_ge(s_gat, t + 1)
                mark(v.tensor_copy(gaT[:, 0:R], ps[0:RANK, 0, 0:R]), s_gate, t + 1)
                v.wait_ge(s_z, t + 1)
                mark(v.tensor_tensor(z_buf[0:R], ps[0:R, 0, 0:GK_W], gate_bias[0:R, :], ALU.add), s_ze, t + 1)
                v.wait_ge(s_l, t + 1)
                if t:
                    v.wait_ge(s_gx, t)
                mark(v.scalar_tensor_tensor(out=ls_buf[0:R], in0=z_buf[0:R], scalar=0.0, in1=ex[0:R, 2],
                                            op0=ALU.min, op1=ALU.subtract), s_ls, t + 1)
                v.wait_ge(s_gxe, t + 1)
                q, k = proj[0:R, t, C_GQ:C_GQ + GK_W], proj[0:R, t, C_GK:C_GK + GK_W]
                sc = GK ** -0.5
                step(v.scalar_tensor_tensor(out=gated[0:R, t, 0], in0=q, scalar=sc, in1=ex[0:R, 2], op0=ALU.mult, op1=ALU.mult))
                step(v.tensor_tensor(gated[0:R, t, 1], k, ex[0:R, 3], ALU.mult))
                step(v.scalar_tensor_tensor(out=q, in0=q, scalar=sc, in1=ex[0:R, 0], op0=ALU.mult, op1=ALU.mult))
                mark(v.tensor_tensor(k, k, ex[0:R, 1], ALU.mult), s_gm, t + 1)
            step(v.memset(s_gla[:, 0], 0.0))
            for t in range(NT):
                R = ROWS[t]
                v.wait_ge(s_gs, t + 1)
                m = K("maskg", P) if t < PT else K("maskg_s", NS)
                for odd in range(2):
                    o = v.tensor_tensor(p_gla[0:R, odd:H:2, 0:R],
                                        ps[0:R, GS_BANK[odd]].rearrange("p (h r) -> p h r", h=H)[:, odd:H:2, 0:R],
                                        m.unsqueeze(1).broadcast_to([R, HP, R]), ALU.mult)
                    if odd:
                        mark(o, s_gp, t + 1)
                    else:
                        step(o)
                if t < PT:
                    for c in range(2):
                        n = 2 * t + c
                        v.wait_ge(s_kv, n + 1)
                        for hh in range(2):
                            rows = slice(hh * GK, (hh + 1) * GK)
                            for hp in range(HP):
                                o = v.scalar_tensor_tensor(
                                    out=s_gla[rows, n + 1, hp], in0=s_gla[rows, n, hp], scalar=dec[rows, hp, n:n + 1],
                                    in1=ps[rows, 6, (2 * hp + hh) * DV:(2 * hp + hh + 1) * DV], op0=ALU.mult, op1=ALU.add)
                                if hh == 1 and hp == HP - 1:
                                    mark(o, s_sg, n + 1)
                                else:
                                    step(o)
                else:
                    v.wait_ge(s_gte, 2 * NT)
                    for hp in range(HP):
                        mark(v.tensor_tensor(qm_g[:, hp], glT[:, 2, hp, 0:NS].unsqueeze(1).broadcast_to([P, SB, NS]),
                                             K("seq_cols").rearrange("p (b n) -> p b n", b=SB), ALU.mult), s_qm, hp + 1)
                    for h in range(H):
                        rows, hp = slice((h % 2) * GK, (h % 2 + 1) * GK), h // 2
                        if h:
                            v.wait_ge(s_gkv, 2 * h)
                        mark(v.tensor_tensor(v_by_seq_g,
                                             proj[0:NS, PT, C_GV + h * DV:C_GV + (h + 1) * DV].unsqueeze(1).broadcast_to([NS, SB, DV]),
                                             K("seq_rows", NS).unsqueeze(2).broadcast_to([NS, SB, DV]), ALU.mult), s_gvs, h + 1)
                        v.wait_ge(s_go, NT)
                        for half in range(2):
                            st = s0_gla[rows, half * 4:half * 4 + 4, hp, :]
                            step(v.tensor_tensor(st, st, dec_s[rows, hp, half * 4:half * 4 + 4].unsqueeze(2).broadcast_to([GK, 4, DV]), ALU.mult))
                            v.wait_ge(s_gkv, 2 * h + half + 1)
                            mark(v.tensor_tensor(st, st, ps[rows, 6].rearrange("p (b v) -> p b v", b=4), ALU.add),
                                 s_gkve, 2 * h + half + 1)
            v.wait_ge(s_roe, H)
            v.wait_ge(s_rsoe, H)
            v.wait_ge(s_goe, NT)
            v.wait_ge(s_hw, 48)
            for t in range(NT):
                R = ROWS[t]
                o = proj[0:R, t, C_RQ:C_RQ + RET_W].rearrange("p (h v) -> p h v", h=H)
                step(v.tensor_reduce(head_mu[0:R], o, AX.X, ALU.add))
                step(v.tensor_scalar(head_mu[0:R], head_mu[0:R], 1.0 / DV, None, ALU.mult))
                mark(v.tensor_tensor(o, o, head_mu[0:R].unsqueeze(2).broadcast_to([R, H, DV]), ALU.subtract), s_nq, t + 1)
            for t in range(NT):
                R = ROWS[t]
                v.wait_ge(s_sq, t + 1)
                mark(v.tensor_reduce(head_ss[0:R, t], proj[0:R, t, C_RK:C_RK + 2 * RET_W].rearrange("p (h v) -> p h v", h=2 * H), AX.X, ALU.add), s_nv, t + 1)
            for t in range(NT):
                R = ROWS[t]
                v.wait_ge(s_nr, t + 1)
                v.wait_ge(s_ng, t + 1)
                for n, (at, gate) in enumerate(((C_RQ, C_RG), (C_GO, C_GG))):
                    o = proj[0:R, t, at:at + RET_W]
                    o3 = o.rearrange("p (h v) -> p h v", h=H)
                    step(v.tensor_tensor(o3, o3, head_rs[0:R, t, n * H:(n + 1) * H].unsqueeze(2).broadcast_to([R, H, DV]), ALU.mult))
                    step(v.tensor_tensor(o, o, head_w[0:R, 2 * n], ALU.mult))
                    if n == 0:
                        step(v.tensor_tensor(o, o, head_w[0:R, 1], ALU.add))
                        step(v.tensor_tensor(o, o, proj[0:R, t, gate:gate + RET_W], ALU.mult))
                    else:
                        mark(v.tensor_tensor(o, o, proj[0:R, t, gate:gate + RET_W], ALU.mult), s_nd, t + 1)
            v.wait_ge(s_mt, 2 * NT)
            step(v.memset(taken[:, PT, :], 0.0))
            step(v.memset(info_tab, 0.0))
            step(v.memset(zeros[:, :], 0.0))
            step(v.memset(gsc[:, 0:TOPG], 1.0e30))
            v.wait_ge(s_bc_ev, 12)
            for t in range(NT):
                R = ROWS[t]
                o = 0 if t < PT else 3
                v.wait_ge(s_r1, t + 1)
                v.wait_ge(s_xr[t % 2], 16 * (t // 2 + 1))
                step(v.scalar_tensor_tensor(out=x1[0:R, t].rearrange("p (c n) -> p c n", c=2),
                                            in0=ps[0:R, 2 * (t % 2):2 * (t % 2) + 2], scalar=rstd[0:R, 1, t:t + 1],
                                            in1=bc2[0:R, o].rearrange("p (c n) -> p c n", c=2), op0=ALU.mult, op1=ALU.mult))
                mark(v.tensor_tensor(x1[0:R, t], x1[0:R, t], x_buf[0:R, t % 2], ALU.add), s_x1, t + 1)
                v.wait_ge(s_r2, t + 1)
                if t >= 2:
                    v.wait_ge(s_h2t, 2 * (t - 1))
                    v.wait_ge(s_h2d[t % 2], 16 * (t // 2))
                tmp = bc2_tmp[0:R]
                step(v.scalar_tensor_tensor(out=tmp, in0=x1[0:R, t], scalar=rstd[0:R, 2, t:t + 1], in1=bc2[0:R, o + 1],
                                            op0=ALU.mult, op1=ALU.mult))
                mark(v.tensor_tensor(h2_buf[0:R, t % 2].rearrange("q (k p) -> q k p", k=KT),
                                     tmp.rearrange("q (p k) -> q k p", k=KT),
                                     bc2[0:R, o + 2].rearrange("q (p k) -> q k p", k=KT), ALU.add), s_h2, t + 1)
            for t in range(NT):
                R = ROWS[t]
                v.wait_ge(s_sig, t + 1)
                sc, se = scores[0:R], sel[0:R]
                step(v.tensor_tensor(se, sc, r_bias[0:R], ALU.add))
                for n in range(G):
                    step(v.max(out=top8[0:R, n], in_=se[:, n * 8:(n + 1) * 8]))
                step(v.tensor_tensor(gsc[0:R, TOPG:], top8[0:R, :, 0], top8[0:R, :, 1], ALU.add))
                step(v.max(out=m8[0:R], in_=gsc[0:R]))
                step(v.match_replace(out=gsc2[0:R], in_to_replace=m8[0:R], in_values=gsc[0:R], imm_value=-1.0e30))
                step(v.tensor_tensor(gsc2[0:R, TOPG:], gsc2[0:R, TOPG:], gsc[0:R, TOPG:], ALU.not_equal))
                gm = gsc2[0:R, TOPG:].unsqueeze(2).broadcast_to([R, G, E // G])
                se3 = se.rearrange("p (g n) -> p g n", g=G)
                step(v.tensor_tensor(se3, se3, gm, ALU.mult))
                step(v.tensor_scalar(gsc2[0:R, TOPG:], gsc2[0:R, TOPG:], 1.0e30, -1.0e30, ALU.mult, ALU.add))
                step(v.tensor_tensor(se3, se3, gm, ALU.add))
                step(v.max(out=m8[0:R], in_=se))
                step(v.match_replace(out=sel2[0:R], in_to_replace=m8[0:R], in_values=se, imm_value=-3.0e38))
                tk = taken[0:R, t]
                step(v.tensor_tensor(tk, sel2[0:R], se, ALU.not_equal))
                step(v.tensor_tensor(sel2[0:R], sc, tk, ALU.mult))
                step(v.tensor_reduce(wsum[0:R, 0:1], sel2[0:R], AX.X, ALU.add))
                step(v.reciprocal(wsum[0:R, 1:2], wsum[0:R, 0:1]))
                inf = info_tab[0:R].rearrange("p (e t c) -> p e t c", e=ECOL, t=NT)[:, 0:E, t]
                step(v.tensor_scalar(inf[:, :, 2], sel2[0:R], wsum[0:R, 1:2], SCALE, ALU.mult, ALU.mult))
                step(v.tensor_scalar(inf[:, :, 0], tk, 0.0, K("tok", R)[:, t:t + 1], ALU.mult, ALU.add))
                step(v.tensor_tensor_scan(sel2[0:R], tk, zeros[0:R], 0.0, ALU.add, ALU.add))
                mark(v.tensor_scalar(inf[:, :, 1], sel2[0:R], K("tok8", R)[:, t:t + 1], None, ALU.add), s_tk, t + 1)
            v.wait_ge(s_pos, 1)
            pt = pos_tab.rearrange("p (c e t) -> p c e t", c=MAXC, e=ECOL)
            step(v.memset(pos_tab, -FAR))
            step(v.tensor_scalar(taken_far[:, :, :], taken[:, :, :], FAR, -FAR, ALU.mult, ALU.add))
            step(v.tensor_tensor(pt[:, 0, 0:E, :].rearrange("p e t -> p t e"), taken_far[:, :, :],
                                 ps[:, 0, 0:NT * E].rearrange("p (t e) -> p t e", t=NT), ALU.add))
            for c in range(1, MAXC):
                step(v.tensor_scalar(pt[:, c, 0:E, :], pt[:, 0, 0:E, :], -float(c * T), None, ALU.add))
            cnt, nb = blocks_e[:, 0:1], blocks_e[:, 1:2]
            step(v.tensor_copy(cnt, ps[0:E, 1, 0:1]))
            step(v.tensor_scalar(nb, cnt, 0.0, None, ALU.is_gt))
            for c in range(1, MAXC):
                o = v.scalar_tensor_tensor(out=nb, in0=cnt, scalar=float(c * T), in1=nb, op0=ALU.is_gt, op1=ALU.add)
                if c < MAXC - 1:
                    step(o)
                else:
                    mark(o, s_blk, 1)
            v.wait_ge(s_pend, 1)
            step(v.tensor_copy(blocks_e[:, 2:3], ps[0:E, 2, 0:1]))
            mark(v.tensor_scalar(in_reach[:, :], K("count", E), blocks_e[:, 2:3], None, ALU.is_ge), s_rch, 1)
            v.wait_ge(s_trow, 1)
            e_row, c_row, n_row = rowf[:, 0], rowf[:, 1], rowf[:, 2]
            step(v.tensor_copy(e_row, ps[0:1, 3, 0:P]))
            step(v.tensor_tensor(c_row, K("count", 1), ps[0:1, 3, P:2 * P], ALU.subtract))
            step(v.tensor_scalar(c_row, c_row, float(MAXC - 1), None, ALU.min))
            step(v.scalar_tensor_tensor(out=c_row, in0=c_row, scalar=float(ECOL), in1=e_row, op0=ALU.mult, op1=ALU.add))
            step(v.tensor_scalar(tab[:, 0], c_row, float(NT), None, ALU.mult))
            step(v.tensor_scalar(tab[:, 1], e_row, float(NT * 3), None, ALU.mult))
            step(v.tensor_scalar(tab[:, 2], e_row, float(E - 1), None, ALU.min))
            step(v.tensor_copy(rowf[:, 3, 0:1], ps[0:1, 3, 2 * P:2 * P + 1]))
            step(v.tensor_scalar(n_row, K("count", 1), float(U), rowf[:, 3, 0:1], ALU.mult, ALU.is_lt))
            step(v.tensor_reduce(rowf[:, 4, 0:1], n_row, AX.X, ALU.add))
            step(v.tensor_scalar(rowf[:, 4, 0:1], rowf[:, 4, 0:1], -1.0, None, ALU.add))
            mark(v.tensor_copy(tab[:, 3, 0:1], rowf[:, 4, 0:1]), s_tab, 1)
            for t in range(NT):
                R = ROWS[t]
                v.wait_ge(s_ssi, t + 1)
                mark(v.tensor_tensor(sh_act[0:R, t].rearrange("q (k p) -> q k p", k=FK),
                                     sh_silu[0:R, t % 2].rearrange("q (p k) -> q k p", k=FK),
                                     ps[0:R, t % 2, FF:2 * FF].rearrange("q (p k) -> q k p", k=FK), ALU.mult), s_sm, t + 1)

            def slots(j, b):
                col = v.value_load(tab[0:1, 0, bass.ds(j, 1)] if not isinstance(j, int) else tab[0:1, 0, j:j + 1],
                                   min_val=0, max_val=(MAXC * ECOL - 1) * NT)
                e = v.value_load(tab[0:1, 1, bass.ds(j, 1)] if not isinstance(j, int) else tab[0:1, 1, j:j + 1],
                                 min_val=0, max_val=E * NT * 3)
                v.tensor_copy(info[:, b % 2], info_tab[:, bass.ds(e, NT * 3)]).then_inc(s_oh, 1)
                v.tensor_tensor(onehot[:, b % 2], K("count")[:, 0:T].unsqueeze(1).broadcast_to([P, NT, T]),
                                pos_tab[:, bass.ds(col, NT)].unsqueeze(2).broadcast_to([P, NT, T]),
                                ALU.is_equal).then_inc(s_oh, 1)

            def slot_info(j, b):
                v.wait_ge(s_info, j + 1)
                at = 3 * j if isinstance(j, int) else j * 3
                v.tensor_copy(slot_info_kept[0:T, bass.ds(at, 3)], ps[0:T, 7, 0:3]).then_inc(s_kept, 1)
                v.tensor_scalar(token_idx[0:T, b:b + 1], ps[0:T, 7, 0:1], EMPTY, None, ALU.add).then_inc(s_idx, 1)

            def row_and_weight(j, b):
                v.wait_ge(s_kept, j + 1)
                at = 3 * j if isinstance(j, int) else j * 3
                v.tensor_copy(slot_w[0:T, b:b + 1], slot_info_kept[0:T, bass.ds(at + 2, 1)]).then_inc(s_wt, 1)
                v.tensor_scalar(row_idx[0:T, b:b + 1], slot_info_kept[0:T, bass.ds(at + 1, 1)], EMPTY, None,
                                ALU.add).then_inc(s_wt, 1)

            def act(j, b):
                v.wait_ge(s_si, j + 1)
                v.tensor_tensor(act_rows[0:T, b % 2].rearrange("q (k p) -> q k p", k=FK),
                                silu_g[0:T, b % 2].rearrange("q (p k) -> q k p", k=FK),
                                ps[0:T, b % 2, FF:2 * FF].rearrange("q (p k) -> q k p", k=FK), ALU.mult).then_inc(s_act, 1)

            def act_T(j, b):
                v.wait_ge(s_at, j + 1)
                v.tensor_copy(actT[:, b % 2], ps[:, 6, 0:FK * T].rearrange("p (k r) -> p k r", k=FK)).then_inc(s_ate, 1)

            def x_high(j, b):
                v.wait_ge(s_xt, j + 1)
                v.tensor_copy(xT[:, b % 2, 4:8, :], ps[:, 5, 0:4 * T].rearrange("p (k r) -> p k r", k=4)).then_inc(s_xtv, 1)

            v.wait_ge(s_sye, NT)
            v.wait_ge(s_h2d[0], 48)
            v.wait_ge(s_h2d[1], 32)
            for j in range(AHEAD):
                slots(j, j)
                slot_info(j, j)
            row_and_weight(0, 0)
            x_high(0, 0)
            act(0, 0)
            act_T(0, 0)
            x_high(1, 1)

            def turn(i, is_last):
                for b in range(U):
                    if not is_last or b + 1 < U:
                        act(i * U + (b + 1), b + 1)
                    if not is_last or b + 2 < U:
                        x_high(i * U + (b + 2), b + 2)
                    if not is_last or b + AHEAD < U:
                        slots(i * U + (b + AHEAD), b + AHEAD)
                    v.wait_ge(s_y, i * U + (b + 1))
                    v.wait_ge(s_wt, i * (2 * U) + (2 * b + 2))
                    v.wait_ge(s_free, i * U + (b + 1))
                    v.tensor_scalar(y_rows[0:T, b % 2, 512:1024], ps[0:T, 3], slot_w[0:T, b:b + 1], None, ALU.mult).then_inc(s_yv, 1)
                    if not is_last or b + 1 < U:
                        act_T(i * U + (b + 1), b + 1)
                        row_and_weight(i * U + (b + 1), (b + 1) % U)
                    if not is_last or b + AHEAD < U:
                        slot_info(i * U + (b + AHEAD), (b + AHEAD) % U)

            last = last_turn(v)
            with v.Fori(0, last) as i:
                turn(i, False)
            turn(last, True)
            for t in range(NT):
                R = ROWS[t]
                o = t // PT
                v.wait_ge(s_yb[t % 2], 16 * (t // 2 + 1))
                y = y_buf[t % 2][0:R]
                step(v.tensor_tensor(y[:, 0:4], y[:, 0:4], y[:, 4:8], ALU.add))
                step(v.tensor_tensor(y[:, 0:2], y[:, 0:2], y[:, 2:4], ALU.add))
                step(v.tensor_tensor(y[:, 0], y[:, 0], y[:, 1], ALU.add))
                mark(v.tensor_tensor(y[:, 0], y[:, 0], shared[0:R, t], ALU.add), s_add, t + 1)
                v.wait_ge(s_r3, t + 1)
                if t >= 2:
                    v.wait_ge(s_out, 16 * (2 + 2 * H + t - 1))
                ob = out_buf[0:R, t % 2]
                step(v.scalar_tensor_tensor(out=ob, in0=y[:, 0], scalar=rstd[0:R, 3, t:t + 1], in1=bcg2[0:R, o],
                                            op0=ALU.mult, op1=ALU.mult))
                mark(v.tensor_tensor(ob, ob, x1[0:R, t], ALU.add), s_fin, t + 1)

        @block.tensor
        def _(pe):
            pe.wait_ge(s_const, 16)
            pe.wait_ge(s_silu, 1)
            for k in range(KT):
                o = pe.transpose(ps[:, 0, k * NCOND:(k + 1) * NCOND], cond[:, k * P:(k + 1) * P], ident[0:NCOND, 0:NCOND])
            o.then_inc(s_cT, 1)
            pe.wait_ge(s_cTs, 1)
            with pe.Fori(0, 6) as i:
                for b in range(2):
                    pe.wait_ge(s_wada[b], 16 * i + 16)
                    pe.wait_ge(s_mod_ev, 2 * i + b + 1)
                    for k in range(KT):
                        o = pe.matmul(ps[0:NCOND, b], condT[:, k, :], w_ada_buf[:, b, k], start=(k == 0), stop=(k == KT - 1))
                    o.then_inc(s_mod, 1)

            pe.wait_ge(s_fold, 4)

            def broadcast(col, sample, bank):
                sel_rows = K("sels", NCOND) if sample else K("selp", NCOND)
                R = NS if sample else P
                for half in range(2):
                    o = pe.matmul(ps[0:R, bank + half], sel_rows, mod[0:NCOND, col * D + half * 512:col * D + half * 512 + 512],
                                  start=True, stop=True)
                o.then_inc(s_bc, 1)

            for n, (col, sample) in enumerate(((1, 0), (0, 0), (1, 1), (0, 1))):
                broadcast(col, sample, 2 * n)
            pe.wait_ge(s_bc_ev, 4)

            def transpose_rows(src, t, banks, done, free, ahead, base=0):
                R = ROWS[t]
                for half in range(2):
                    n = 2 * t + half
                    if n >= ahead:
                        pe.wait_ge(free, base + n - ahead + 1)
                    for k in range(4):
                        kk = 4 * half + k
                        o = pe.transpose(ps[:, banks + n % ahead, k * P:k * P + R], src(kk), ident[0:R, 0:R])
                    o.then_inc(done, 1)

            for t in range(NT):
                pe.wait_ge(s_h, t + 1)
                transpose_rows(lambda k: h_buf[0:ROWS[t], t % 2, k * P:(k + 1) * P], t, 0, s_tr, s_hT, 4)
            pe.wait_ge(s_hT, 2 * NT)
            with pe.Fori(0, 4) as i:
                for b in range(2):
                    pe.wait_ge(s_win[b], 16 * i + 16)
                    for t in range(NT):
                        pe.wait_ge(s_pj_ev, (2 * i + b) * NT + t + 1)
                        for k in range(KT):
                            o = pe.matmul(ps[0:ROWS[t], t, 0:GW], hT[:, k, t * P:t * P + ROWS[t]], w_in_buf[:, b, k],
                                          start=(k == 0), stop=(k == KT - 1))
                        o.then_inc(s_pj, 1)
            pe.wait_ge(s_pj_ev, 9 * NT)
            for t in range(NT):
                pe.wait_ge(s_rot, t + 1)
                transpose_rows(lambda k: proj[0:ROWS[t], t, k * P:(k + 1) * P], t, 0, s_rtr, s_qkT, 4)
            pe.wait_ge(s_qkT, 2 * NT)
            pe.wait_ge(s_ks, NT)
            pe.wait_ge(s_st, 16 * (1 + H))
            for h in range(H):
                for J in range(PT):
                    n = SEQ - J * P
                    if PT * h + J >= 2:
                        pe.wait_ge(s_p, PT * h + J - 1)
                    pe.matmul(ps[:, 4 + J % 2, 0:n], qkT[:, H + h, J * P:(J + 1) * P], qkT[:, h, J * P:SEQ],
                              start=True, stop=True).then_inc(s_sc, 1)
                if h:
                    pe.wait_ge(s_rp, h)
                pe.matmul(ps[0:NS, 1, 0:NS], qkT[:, H + h, SEQ:N], qkT[:, h, SEQ:N], start=True, stop=True).then_inc(s_rsc, 1)
                for J in range(PT):
                    o = pe.matmul(ps[:, 0, h * DV:(h + 1) * DV], proj[:, J, C_RK + h * DK:C_RK + (h + 1) * DK],
                                  proj[:, J, C_RV + h * DV:C_RV + (h + 1) * DV], start=(J == 0), stop=(J == PT - 1))
                if h == H - 1:
                    o.then_inc(s_rst, 1)
                pe.wait_ge(s_p, PT * (h + 1))
                if h >= 2:
                    pe.wait_ge(s_roe, h - 1)
                for I in range(PT):
                    for J in range(I + 1):
                        at = PR_OFF[J] + (I - J) * P
                        o = pe.matmul(ps[:, 6 + h % 2, I * DV:(I + 1) * DV], pr[:, h % 2, at:at + P],
                                      proj[:, J, C_RV + h * DV:C_RV + (h + 1) * DV], start=(J == 0), stop=(J == I))
                o.then_inc(s_ro, 1)
                pe.wait_ge(s_rp, h + 1)
                if h:
                    pe.wait_ge(s_rsoe, h)
                pe.matmul(ps[0:NS, 2, 0:DV], pr_s, proj[0:NS, PT, C_RV + h * DV:C_RV + (h + 1) * DV], start=True, stop=False)
                for b in range(SB):
                    o = pe.matmul(ps[0:NS, 2, 0:DV], qm_r[:, b], s0_ret[:, b, h], start=False, stop=(b == SB - 1))
                o.then_inc(s_rso, 1)
                pe.wait_ge(s_vs, h + 1)
                for half in range(2):
                    if 2 * h + half:
                        pe.wait_ge(s_rkve, 2 * h + half)
                    pe.matmul(ps[:, 3], proj[0:NS, PT, C_RK + h * DK:C_RK + (h + 1) * DK],
                              v_by_seq[:, half * 4:half * 4 + 4].rearrange("p b v -> p (b v)"), start=True, stop=True).then_inc(s_rkv, 1)
            pe.wait_ge(s_rste, 1)
            for t in range(NT):
                R = ROWS[t]
                sfx = "" if t < PT else "_s"
                if t:
                    pe.wait_ge(s_ze, t)
                pe.transpose(ps[0:RANK, 0, 0:R], proj[0:R, t, C_GA:C_GA + RANK], ident[0:R, 0:R]).then_inc(s_gat, 1)
                pe.wait_ge(s_gate, t + 1)
                pe.matmul(ps[0:R, 0, 0:GK_W], gaT[:, 0:R], gate_up[:, :], start=True, stop=True).then_inc(s_z, 1)
                pe.wait_ge(s_ls, t + 1)
                if t:
                    pe.wait_ge(s_gxe, t)
                pe.matmul(ps[0:R, 1, 0:GK_W], K("gmid" + sfx, R), ls_buf[0:R], start=True, stop=True)
                pe.matmul(ps[0:R, 1, GK_W:2 * GK_W], K("gcum" + sfx, R), ls_buf[0:R], start=True, stop=True)
                pe.matmul(ps[0:R, 2, 0:GK_W], K("gend" + sfx, R), ls_buf[0:R], start=True, stop=True)
                nc_ = 2 if t < PT else SB
                for hp in range(HP):
                    o = pe.matmul(ps[:, 2, GK_W + hp * nc_:GK_W + (hp + 1) * nc_], ls_buf[0:R, hp * P:(hp + 1) * P],
                                  K("chunk" + sfx, R), start=True, stop=True)
                o.then_inc(s_gx, 1)
            for t in range(NT):
                R = ROWS[t]
                pe.wait_ge(s_gm, t + 1)
                if t == 0:
                    pe.wait_ge(s_gxe, NT)
                for n in range(2):
                    if t:
                        pe.wait_ge(s_gte, 2 * (t - 1) + n + 1)
                    for w, src in enumerate((proj[0:R, t, C_GQ:C_GQ + GK_W], proj[0:R, t, C_GK:C_GK + GK_W], gated[0:R, t, 0])):
                        o = pe.transpose(ps[:, 3 + n, w * P:w * P + R], src[:, n * P:(n + 1) * P], ident[0:R, 0:R])
                    o.then_inc(s_gt, 1)
                pe.wait_ge(s_gte, 2 * t + 2)
                if t:
                    pe.wait_ge(s_gp, t)
                for h in range(H):
                    rows, hp = slice((h % 2) * GK, (h % 2 + 1) * GK), h // 2
                    o = pe.matmul(ps[0:R, GS_BANK[h % 2], h * P:h * P + R], glT[rows, 1, hp, 0:R], glT[rows, 0, hp, 0:R], start=True, stop=True)
                o.then_inc(s_gs, 1)
                if t < PT:
                    for c in range(2):
                        n = 2 * t + c
                        if n:
                            pe.wait_ge(s_sg, n)
                        crow = slice(c * CH, (c + 1) * CH)
                        for hp in range(HP):
                            o = pe.matmul(ps[:, 6, 2 * hp * DV:2 * (hp + 1) * DV], gated[crow, t, 1, hp * P:(hp + 1) * P],
                                          proj[crow, t, C_GV + 2 * hp * DV:C_GV + 2 * (hp + 1) * DV], start=True, stop=True)
                        o.then_inc(s_kv, 1)
                pe.wait_ge(s_gp, t + 1)
                if t:
                    pe.wait_ge(s_goe, t)
                if t < PT:
                    pe.wait_ge(s_sg, 2 * t + 1)
                else:
                    pe.wait_ge(s_qm, HP)
                for h in range(H):
                    rows, hp = slice((h % 2) * GK, (h % 2 + 1) * GK), h // 2
                    out = ps[0:R, GO_BANK[h % 2], h * DV:(h + 1) * DV]
                    o = pe.matmul(out, p_gla[0:R, h, 0:R], proj[0:R, t, C_GV + h * DV:C_GV + (h + 1) * DV], start=True, stop=False)
                    if t == PT and h % 2:
                        o.then_inc(s_rowtile, 1)
                        pe.wait_ge(s_rowtile, h)
                    if t < PT:
                        for c in range(2):
                            o = pe.matmul(ps[c * CH:(c + 1) * CH, GO_BANK[h % 2], h * DV:(h + 1) * DV], glT[rows, 2, hp, c * CH:(c + 1) * CH],
                                          s_gla[rows, 2 * t + c, hp], start=False, stop=True)
                    else:
                        for b in range(SB):
                            o = pe.matmul(out, qm_g[rows, hp, b], s0_gla[rows, b, hp], start=False, stop=(b == SB - 1))
                        if h == 1:
                            o.then_inc(s_rowtile, 1)
                            pe.wait_ge(s_rowtile, 2)
                o.then_inc(s_go, 1)
            for h in range(H):
                hp = h // 2
                pe.wait_ge(s_gvs, h + 1)
                for half in range(2):
                    if 2 * h + half:
                        pe.wait_ge(s_gkve, 2 * h + half)
                    pe.matmul(ps[:, 6], gated[0:NS, PT, 1, hp * P:(hp + 1) * P],
                              v_by_seq_g[:, half * 4:half * 4 + 4].rearrange("p b v -> p (b v)"), start=True, stop=True).then_inc(s_gkv, 1)
            pe.wait_ge(s_goe, NT)
            pe.wait_ge(s_gkve, 2 * H)
            pe.wait_ge(s_out, 16 * (2 + 2 * H))
            for n, (col, sample) in enumerate(((2, 0), (4, 0), (3, 0), (2, 1), (4, 1), (3, 1), (5, 0), (5, 1))):
                if n >= 2:
                    pe.wait_ge(s_bc_ev, 4 + n - 1)
                m = n if n < 6 else n - 6
                broadcast(col, sample, 4 + 2 * (m % 2))
            for t in range(NT):
                pe.wait_ge(s_nd, t + 1)
                transpose_rows(lambda k: proj[0:ROWS[t], t, (C_RQ + k * P) if k < 4 else (C_GO + (k - 4) * P):
                                              (C_RQ + k * P + P) if k < 4 else (C_GO + (k - 4) * P + P)],
                               t, 0, s_mt, s_mte, 4)
            pe.wait_ge(s_mte, 2 * NT)
            pe.wait_ge(s_wout, 16)
            pe.wait_ge(s_bc_ev, 12)
            for t in range(NT):
                if t >= 2:
                    pe.wait_ge(s_x1, t - 1)
                for half in range(2):
                    for k in range(KT):
                        o = pe.matmul(ps[0:ROWS[t], 2 * (t % 2) + half], hT[:, k, t * P:t * P + ROWS[t]],
                                      w_out_buf[:, k, half * 512:half * 512 + 512], start=(k == 0), stop=(k == KT - 1))
                o.then_inc(s_wo, 1)
                if t >= 1:
                    pe.wait_ge(s_h2, t)
                    transpose_rows(lambda k: h2_buf[0:ROWS[t - 1], (t - 1) % 2, k * P:(k + 1) * P], t - 1, 4, s_h2t, s_h2T, 2)
            pe.wait_ge(s_h2, NT)
            transpose_rows(lambda k: h2_buf[0:NS, PT % 2, k * P:(k + 1) * P], PT, 4, s_h2t, s_h2T, 2)
            pe.wait_ge(s_h2T, 2 * NT)
            for t in range(NT):
                if t >= 2:
                    pe.wait_ge(s_sig, t - 1)
                for k in range(KT):
                    o = pe.matmul(ps[0:ROWS[t], 6 + t % 2, 0:E], hT[:, k, t * P:t * P + ROWS[t]], w_router_buf[:, k, :],
                                  start=(k == 0), stop=(k == KT - 1))
                o.then_inc(s_lg, 1)
            pe.wait_ge(s_tk, NT)
            for t in range(NT):
                for u in range(t):
                    pe.matmul(ps[:, 0, t * E:(t + 1) * E], K("ones"), taken[:, u], start=(u == 0), stop=False)
                pe.matmul(ps[:, 0, t * E:(t + 1) * E], K("before"), taken[:, t], start=(t == 0), stop=True)
            for t in range(NT):
                o = pe.matmul(ps[0:E, 1, 0:1], taken[:, t], K("ones")[:, 0:1], start=(t == 0), stop=(t == NT - 1))
            o.then_inc(s_pos, 1)
            pe.wait_ge(s_blk, 1)
            pe.matmul(ps[0:E, 2, 0:1], K("upto", E), blocks_e[:, 1:2], start=True, stop=True).then_inc(s_pend, 1)
            pe.wait_ge(s_rch, 1)
            pe.matmul(ps[0:1, 3, 0:P], K("ones", E)[:, 0:1], in_reach, start=True, stop=True)
            pe.matmul(ps[0:1, 3, P:2 * P], blocks_e[:, 1:2], in_reach, start=True, stop=True)
            pe.matmul(ps[0:1, 3, 2 * P:2 * P + 1], blocks_e[:, 1:2], K("ones", E)[:, 0:1], start=True, stop=True).then_inc(s_trow, 1)
            pe.wait_ge(s_wsh, 48)
            for t in range(NT):
                if t >= 2:
                    pe.wait_ge(s_sm, t - 1)
                if t == 0:
                    pe.wait_ge(s_tab, 1)
                for k in range(KT):
                    o = pe.matmul(ps[0:ROWS[t], t % 2], hT[:, k, t * P:t * P + ROWS[t]], w_sh[:, k], start=(k == 0), stop=(k == KT - 1))
                o.then_inc(s_sgu, 1)
            for t in range(NT):
                R = ROWS[t]
                pe.wait_ge(s_sm, t + 1)
                if t >= 2:
                    pe.wait_ge(s_shte, t - 1)
                for k in range(FK):
                    o = pe.transpose(ps[:, 2 + t % 2, k * P:k * P + R], sh_act[0:R, t, k * P:(k + 1) * P], ident[0:R, 0:R])
                o.then_inc(s_sht, 1)
            for t in range(NT):
                R = ROWS[t]
                pe.wait_ge(s_shte, t + 1)
                if t >= 2:
                    pe.wait_ge(s_sye, t - 1)
                for half in range(2):
                    for k in range(FK):
                        o = pe.matmul(ps[0:R, 4 + 2 * (t % 2) + half], sh_actT[:, t, k, 0:R],
                                      w_sh_down_buf[:, k, half * 512:half * 512 + 512], start=(k == 0), stop=(k == FK - 1))
                o.then_inc(s_sy, 1)

            def slot_info(j, b):
                pe.wait_ge(s_oh, j * 2 + 2)
                if not (isinstance(j, int) and j < 1):
                    pe.wait_ge(s_idx, j)
                    pe.wait_ge(s_kept, j)
                for t in range(NT):
                    o = pe.matmul(ps[0:T, 7, 0:3], onehot[:, b % 2, t], info[:, b % 2, t * 3:(t + 1) * 3],
                                  start=(t == 0), stop=(t == NT - 1))
                o.then_inc(s_info, 1)

            def x_transposed(i, b):
                pe.wait_ge(s_xg[b % 2], 16 * (i * (U // 2) + (b // 2 + 1)))
                for k in range(KT):
                    o = pe.transpose(ps[:, 4 + k // 4, (k % 4) * T:(k % 4 + 1) * T], x_rows[0:T, b % 2, k * P:(k + 1) * P],
                                     ident[0:T, 0:T])
                o.then_inc(s_xt, 1)

            def gate_up_mm(j, b, turns):
                pe.wait_ge(s_wgu[b % U], 32 * turns)
                pe.wait_ge(s_xta, j + 1)
                pe.wait_ge(s_xtv, j + 1)
                for k in range(KT):
                    o = pe.matmul(ps[0:T, b % 2], xT[:, b % 2, k], w_gu[b % RING][:, :, k, :], start=(k == 0), stop=(k == KT - 1))
                o.then_inc(s_gu, 1)

            def act_transposed(j, b):
                pe.wait_ge(s_act, j + 1)
                for k in range(FK):
                    o = pe.transpose(ps[:, 6, k * T:(k + 1) * T], act_rows[0:T, b % 2, k * P:(k + 1) * P], ident[0:T, 0:T])
                o.then_inc(s_at, 1)

            def down_mm(j, b, turns):
                pe.wait_ge(s_wdn[b], 16 * turns)
                pe.wait_ge(s_ate, j + 1)
                pe.wait_ge(s_ya, j + 1)
                pe.wait_ge(s_yv, j + 1)
                for half in range(2):
                    for k in range(FK):
                        o = pe.matmul(ps[0:T, 2 + half], actT[:, b % 2, k], w_dn[b % RING][:, k, half * 512:half * 512 + 512],
                                      start=(k == 0), stop=(k == FK - 1))
                o.then_inc(s_y, 1)

            pe.wait_ge(s_sye, NT)
            for j in range(AHEAD):
                slot_info(j, j)
            x_transposed(0, 0)
            gate_up_mm(0, 0, 1)
            act_transposed(0, 0)
            x_transposed(0, 1)

            def turn(i, is_last):
                for b in range(U):
                    if not is_last or b + 1 < U:
                        gate_up_mm(i * U + (b + 1), b + 1, i + ((b + 1) // U + 1))
                    if not is_last or b + 2 < U:
                        x_transposed(i, b + 2)
                    down_mm(i * U + b, b, i + 1)
                    if not is_last or b + 1 < U:
                        act_transposed(i * U + (b + 1), b + 1)
                    if not is_last or b + AHEAD < U:
                        slot_info(i * U + (b + AHEAD), b + AHEAD)

            last = last_turn(pe)
            with pe.Fori(0, last) as i:
                turn(i, False)
            turn(last, True)


def kernel(**inputs):
    import concourse.bacc as bacc
    from concourse.bass_utils import run_bass_kernel_spmd

    nc = bacc.Bacc("TRN2", target_bir_lowering=False, num_devices=1)
    names = ["x_prompt", "x_sample", "state_ret", "state_gla", "c_prompt", "c_sample", "w_ada", "b_ada", "norm_pre_mix",
             "norm_post_mix", "norm_pre_ffn", "norm_post_ffn", "w_in", "gla_gate_up", "gla_gate_bias", "ret_norm_w",
             "ret_norm_b", "gla_norm_w", "w_out", "w_router", "router_bias", "w_exp_gate", "w_exp_up", "w_exp_down",
             "w_sh_gate", "w_sh_up", "w_sh_down"]
    arrays, args = {}, []
    for name in names:
        arrays["in_" + name] = np.ascontiguousarray(inputs[name])
    arrays["in_consts"] = _constants()
    for name in names + ["consts"]:
        a = arrays["in_" + name]
        args.append(nc.dram_tensor("in_" + name, a.shape, mybir.dt.from_np(a.dtype), kind="ExternalInput").ap())
    outs = [("y_prompt", (1, SEQ, D)), ("y_sample", (SB, SS, D)), ("ret_prompt", (1, 1, H, DK, DV)),
            ("gla_prompt", (1, 1, H, GK, DV)), ("ret_sample", (1, SB, H, DK, DV)), ("gla_sample", (1, SB, H, GK, DV))]
    for name, shape in outs:
        args.append(nc.dram_tensor("out_" + name, shape, F32, kind="ExternalOutput").ap())
    args.append(nc.dram_tensor("h2_rows", (N, D), F32, kind="Internal").ap())
    args.append(nc.dram_tensor("expert_rows", (N * TOPK, D), F32, kind="Internal").ap())
    hybrid_step(nc, *args)
    r = run_bass_kernel_spmd(nc, [arrays], core_ids=[0])
    return tuple(r.results[0]["out_" + name] for name, _ in outs)
```

```python
import concourse.bass as bass
from concourse import mybir
from concourse.alu_op_type import AluOpType as ALU
from contextlib import ExitStack
import numpy as np

F32 = mybir.dt.float32
F32R = mybir.dt.float32r
I32 = mybir.dt.int32
U32 = mybir.dt.uint32
ACT = mybir.ActivationFunctionType
AX = mybir.AxisListType

P = 128
D = 1024
KT = D // P
SEQ, SB, SS = 512, 8, 8
NS = SB * SS
N = SEQ + NS
PT = SEQ // P
NT = PT + 1
ROWS = [P] * PT + [NS]
H, DK, GK, DV, RANK = 4, 128, 64, 128, 16
HP = H // 2
CH = 64
NCH = SEQ // CH
RET_W, GK_W = H * DK, H * GK
C_RQ, C_RK, C_RV, C_RG = 0, RET_W, 2 * RET_W, 3 * RET_W
C_GQ = 4 * RET_W
C_GK = C_GQ + GK_W
C_GV = C_GK + GK_W
C_GG = C_GV + RET_W
C_GA = C_GG + RET_W
IN_W = C_GA + RANK
C_GO = C_GQ
E, G, TOPK, TOPG, FF = 64, 8, 8, 4, 256
FK = FF // P
EPS = 1e-6
SCALE = 2.5
PAST = 4096
NCOND = 1 + SB
GAMMA = [1.0 - 2.0 ** (-5.0 - h) for h in range(H)]
EMPTY = 8192.0
FAR = 1.0e6
T = 104
MAXC = -(-N // T)
MAX_BLOCKS = E + N * TOPK // T
MIN_BLOCKS = -(-N * TOPK // T)
ECOL = E + 1
U = 4
RING = 2
AHEAD = 4
GATHER_AHEAD = 3

_consts = {}
_width = 0


def _col(name, n):
    global _width
    _consts[name] = (_width, n)
    _width += n


for _n, _w in [("ident", P), ("ones", P), ("before", P), ("maskg", P), ("gmid", P), ("gcum", P), ("gend", P),
               ("gmid_s", NS), ("gcum_s", NS), ("gend_s", NS), ("maskg_s", NS), ("chunk", 2), ("chunk_s", SB),
               ("dret", H * SEQ), ("dret_s", H * NS), ("cos", NT * 64), ("sin", NT * 64), ("kpow", NT * H),
               ("qpow_s", H * NS), ("seq_cols", SB * NS), ("seq_rows", SB), ("selp", P), ("sels", NS),
               ("upto", E), ("count", P), ("tok", NT), ("tok8", NT)]:
    _col(_n, _w)
CONST_W = _width

MOD0 = CONST_W
PROJ0 = MOD0 + 6 * D
WORK0 = PROJ0 + NT * IN_W
HT0 = WORK0 + 10752
ST0 = HT0 + KT * N
ARENA_W = ST0 + 6 * D
RING_AT = [WORK0, ST0]
W_COLS = (2 * KT * FF, FK * D)


def _constants():
    a = np.zeros((P, CONST_W), np.float32)

    def put(name, v):
        v = np.asarray(v, np.float32)
        v = v.reshape(v.shape[0], -1)
        o, n = _consts[name]
        assert v.shape[1] == n, (name, v.shape, n)
        a[:v.shape[0], o:o + n] = v

    i = np.arange(P)
    put("ident", np.eye(P))
    put("ones", np.ones((P, P)))
    put("before", i[:, None] < i[None, :])

    def gates(size, chunk, suffix):
        j, t = np.arange(size)[:, None], np.arange(size)[None, :]
        same = j // chunk == t // chunk
        mid = t // chunk * chunk + chunk // 2 - 1
        cum = same & (j <= t)
        put("gcum" + suffix, cum / 16.0)
        put("gmid" + suffix, (cum.astype(float) - (same & (j <= mid))) / 16.0)
        put("gend" + suffix, (same & (j > t)) / 16.0)
        put("maskg" + suffix, cum)
        put("chunk" + suffix, (j // chunk == np.arange(size // chunk)[None, :]) / 16.0)

    gates(P, CH, "")
    gates(NS, SS, "_s")
    j, t = np.arange(P)[:, None], np.arange(SEQ)[None, :]
    scale = DK ** -0.5
    put("dret", np.stack([np.where(t >= j, np.float64(g) ** np.maximum(t - j, 0), 0) * scale for g in GAMMA], 1))
    j, t = np.arange(NS)[:, None], np.arange(NS)[None, :]
    put("dret_s", np.stack([np.where((t >= j) & (t // SS == j // SS), np.float64(g) ** np.maximum(t - j, 0), 0) * scale
                            for g in GAMMA], 1))
    half = DK // 2
    inv = (np.float32(10000.0) ** (-np.arange(half, dtype=np.float32) / np.float32(half))).astype(np.float32)
    pos = np.concatenate([np.arange(SEQ), np.tile(PAST + np.arange(SS), SB), np.zeros(P - NS)]).astype(np.float32)
    ang = (pos[:, None] * inv[None, :]).astype(np.float32).reshape(NT, P, half).transpose(1, 0, 2)
    put("cos", np.cos(ang.astype(np.float64)))
    put("sin", np.sin(ang.astype(np.float64)))
    kp = np.zeros((P, NT, H))
    qp = np.zeros((P, H, NS))
    for h, g in enumerate(GAMMA):
        for n in range(PT):
            kp[:, n, h] = np.float64(g) ** (SEQ - 1 - (n * P + i)) * scale
        kp[:NS, PT, h] = np.float64(g) ** (SS - 1 - np.arange(NS) % SS) * scale
        qp[:, h, :] = np.float64(g) ** (np.arange(NS) % SS + 1)
    put("kpow", kp)
    put("qpow_s", qp)
    put("seq_cols", np.broadcast_to(np.arange(NS)[None, None, :] // SS == np.arange(SB)[None, :, None], (P, SB, NS)))
    put("seq_rows", np.arange(NS)[:, None] // SS == np.arange(SB)[None, :])
    put("selp", np.eye(NCOND)[:, [0] * P])
    put("sels", (np.arange(NCOND)[:, None] == 1 + np.arange(NS)[None, :] // SS))
    put("upto", np.arange(E)[:, None] <= np.arange(E)[None, :])
    put("count", np.broadcast_to(i[None, :], (P, P)))
    tok = np.arange(NT)[None, :] * P + i[:, None]
    put("tok", tok - EMPTY)
    put("tok8", tok * TOPK - 1 - EMPTY)
    return a


def hybrid_step(nc, x_prompt, x_sample, state_ret, state_gla, c_prompt, c_sample, w_ada, b_ada, norm_pre_mix,
                norm_post_mix, norm_pre_ffn, norm_post_ffn, w_in, gla_gate_up, gla_gate_bias, ret_norm_w,
                ret_norm_b, gla_norm_w, w_out, w_router, router_bias, w_exp_gate, w_exp_up, w_exp_down, w_sh_gate,
                w_sh_up, w_sh_down, consts, y_prompt, y_sample, ret_p, gla_p, ret_s, gla_s, mod_rows, h2_rows, expert_rows):
    ctx = ExitStack()
    with ctx:
        def sb(name, shape, dt=F32):
            return ctx.enter_context(nc.sbuf_tensor(name, shape, dt))

        def sem(name):
            return ctx.enter_context(nc.semaphore(name))

        def over_arena(name, at, shape):
            with nc.sbuf_tensor(name + "_from", [P, at], F32), nc.sbuf_tensor(name, shape, F32R) as t:
                return t

        GW = 300
        NG = IN_W // GW
        hT_hi = over_arena("hT_hi", HT0, [P, KT, N])
        hT_lo = over_arena("hT_lo", MOD0, [P, KT, N])
        w_hi = [over_arena("w_hi0", WORK0 + KT * GW, [P, KT, GW]), over_arena("w_hi1", ST0, [P, KT, GW])]
        w_lo = [over_arena("w_lo0", WORK0 + 2 * KT * GW, [P, KT, GW]), over_arena("w_lo1", ST0 + KT * GW, [P, KT, GW])]
        down_hi = over_arena("down_hi", MOD0, [P, FK, D])
        down_lo = over_arena("down_lo", MOD0 + FK * D, [P, FK, D])
        actT_hi = over_arena("actT_hi", MOD0 + 2 * FK * D, [P, 2, FK, T])
        actT_lo = over_arena("actT_lo", MOD0 + 2 * FK * D + 2 * FK * T, [P, 2, FK, T])
        arena = ctx.enter_context(nc.sbuf_tensor("arena", [P, ARENA_W], F32))

        def region(at, *dims, rows=P, start=0):
            n = int(np.prod(dims))
            v = arena[start:start + rows, at:at + n]
            if len(dims) == 2:
                return v.rearrange("p (a b) -> p a b", a=dims[0])
            if len(dims) == 3:
                return v.rearrange("p (a b c) -> p a b c", a=dims[0], b=dims[1])
            if len(dims) == 4:
                return v.rearrange("p (a b c d) -> p a b c d", a=dims[0], b=dims[1], c=dims[2])
            return v

        def K(name, rows=P):
            o, n = _consts[name]
            return arena[0:rows, o:o + n]

        ident = K("ident")
        mod = region(MOD0, 6 * D)
        proj = region(PROJ0, NT, IN_W)
        hT = region(HT0, KT, N)
        cond = region(PROJ0, D, rows=NCOND)
        ada_bias = region(PROJ0 + D, 6 * D, rows=NCOND)
        norm_rows = region(PROJ0 + 7 * D, 4, D, rows=NCOND)
        w_ada_buf = region(WORK0, 2, KT, 512)
        condT = sb("condT", [P, KT, NCOND])
        bc1 = region(ST0, 4, D)
        x_buf = region(WORK0 + 8192, 2, D)
        h_buf = region(PROJ0 + 11 * D, 2, D)
        w_in_buf = region(WORK0, KT, GW)
        ss = sb("ss", [P, 4, NT])
        rstd = sb("rstd", [P, 4, NT])
        minus_half = sb("minus_half", [P, 16])
        square_junk = region(PROJ0 + 13 * D, D)
        sq_junk2 = region(PROJ0 + 6 * D, D)
        bc2_tmp = region(PROJ0 + 5 * D, D)
        s0_ret = region(ST0, SB, H, DV)
        s0_gla = region(ST0 + SB * H * DV, SB, HP, DV)
        gate_up = sb("gate_up", [RANK, GK_W])
        gate_bias = sb("gate_bias", [P, GK_W])
        head_w = region(_consts["dret"][0], 3, RET_W)
        head_mu = sb("head_mu", [P, H])
        head_ss = sb("head_ss", [P, NT, 2 * H])
        head_rs = sb("head_rs", [P, NT, 2 * H])
        rot = region(WORK0 + 8192, 4, 2 * H * 64)
        qkT = region(HT0, 2 * H, N)
        pr = region(WORK0 + 2048, 2, 1280)
        PR_OFF = [0, 512, 896, 1152]
        pr_s = region(WORK0 + 4608, NS, rows=NS)
        qm_r = region(WORK0 + 4672, SB, NS)
        qg_r = region(WORK0 + 5184, NS)
        v_by_seq = region(WORK0 + 5248, SB, DV, rows=NS)
        ret_out = region(WORK0 + 6272, H, DV)
        gated = region(WORK0, NT, 2, GK_W)
        glT = region(WORK0 + 2560, 3, HP, P)
        p_gla = region(WORK0 + 3328, H, P)
        s_gla = region(WORK0 + 3840, NCH + 1, HP, DV)
        z_buf = region(WORK0 + 2560, NT, GK_W)
        softplus = region(WORK0 + 3840, NT, GK_W)
        ls_buf = region(WORK0 + 5120, NT, GK_W)
        ex = region(WORK0 + 6656, 2, 4, GK_W)
        qm_g = region(WORK0 + 7680, HP, SB, NS)
        v_by_seq_g = region(WORK0 + 8704, SB, DV, rows=NS)
        gaT = [region(WORK0 + at, P, rows=RANK) for at in (9728, 9888)]
        dec = region(WORK0 + 9856, HP, NCH)
        dec_s = region(WORK0 + 9872, HP, SB)
        w_out_buf = region(WORK0, KT, D)
        bc2 = region(ST0, 6, D)
        x1 = region(PROJ0, NT, D)
        shared = region(PROJ0 + 5 * D, NT, D)
        bcg2 = region(PROJ0 + 10 * D, 2, D)
        pos_tab = region(PROJ0 + 12 * D, MAXC * ECOL * NT)
        info_tab = region(PROJ0 + 12 * D + MAXC * ECOL * NT, ECOL * NT * 3)
        HB0 = PROJ0 + 12 * D + MAXC * ECOL * NT + ECOL * NT * 3
        h2_buf = region(HB0, 2, D)
        w_sh = region(MOD0, KT, 2 * FF)
        w_sh_down_buf = region(MOD0 + KT * 2 * FF, FK, D)
        assert HB0 + 2304 <= WORK0
        w_router_buf = sb("w_router_buf", [P, KT, E])
        r_bias = sb("r_bias", [P, E])
        small_at = [_consts["dret"][0]]

        def small(*dims, rows=P):
            at = small_at[0]
            small_at[0] += int(np.prod(dims))
            assert small_at[0] <= _consts["dret"][0] + H * SEQ
            return region(at, *dims, rows=rows)

        scores, sel, sel2, zeros = small(NT, E), small(E), small(E), small(E)
        top8 = small(G, 8)
        gsc, gsc2 = small(TOPG + G), small(TOPG + G)
        m8 = small(8)
        taken, taken_far = small(NT, E), small(NT, E)
        wsum = small(4)
        blocks_e = small(4, rows=E)
        in_reach = small(P, rows=E)
        rowf = small(5, P, rows=1)
        tab = region(_consts["before"][0] + P, 4, P, rows=1).bitcast(I32)
        onehot = region(HB0, 2, NT, T)
        act_rows = region(HB0 + 1280, 2, FF)
        silu_g = region(WORK0 + 10240, 2, FF)
        w_gu = [region(a, 2, KT, FF) for a in RING_AT]
        w_dn = [region(a + W_COLS[0], FK, D) for a in RING_AT]
        x_rows = region(WORK0 + 6144, 2, D)
        xT = region(WORK0 + 8192, 2, KT, T)
        y_rows = region(HT0, 2, D)
        sh_act = region(WORK0 + 6144, NT, FF)
        sh_silu = region(WORK0 + 6144 + NT * FF, 2, FF)
        sh_actT = region(WORK0 + 6144 + (NT + 2) * FF, NT, FK, P)
        info = sb("info", [P, 2, NT * 3])
        slot_info_kept = sb("slot_info_kept", [P, 3 * (MAX_BLOCKS + U)])
        token_idx = sb("token_idx", [P, U], I32)
        row_idx = sb("row_idx", [P, U], I32)
        slot_w = sb("slot_w", [P, U])
        y_buf = [region(WORK0, TOPK, D), region(HT0, TOPK, D)]
        out_buf = region(MOD0, 2, D)
        sq2 = region(MOD0 + 2 * D, D)
        ps = ctx.enter_context(nc.psum_tensor("ps", [P, 8, 512], F32))

        s_const = sem("consts_in")
        s_cond = sem("cond_in")
        s_rows = sem("rows_in")
        s_small = sem("small_in")
        s_wada = [sem("w_ada_in0"), sem("w_ada_in1")]
        s_silu = sem("cond_silu")
        s_cT = sem("condT_psum")
        s_cTs = sem("condT_ready")
        s_mod = sem("mod_psum")
        s_mod_ev = sem("mod_rows_ready")
        s_fold = sem("mod_folded")
        s_bc = sem("bc_psum")
        s_bc_ev = sem("bc_ready")
        s_x = [sem("x_in0"), sem("x_in1")]
        s_ss = sem("square_sum")
        s_rs = sem("rstd_ready")
        s_h = sem("h_ready")
        s_tr = sem("h_transposed")
        s_hT = sem("hT_ready")
        s_win = sem("w_in_in")
        s_whi = sem("w_in_high_ready")
        s_wlo = sem("w_in_low_ready")
        s_hTl = sem("hT_low_ready")
        s_mst = sem("mod_rows_stored")
        s_bc2 = sem("modulation_again_in")
        s_bcg = sem("last_gate_in")
        s_pj = sem("proj_psum")
        s_pj_ev = sem("proj_ready")
        s_st = sem("states_in")
        s_v = sem("vector_step")
        s_a = sem("scalar_step")
        s_g = sem("gpsimd_step")
        s_rot = sem("rotated")
        s_rtr = sem("qk_transposed")
        s_qkT = sem("qkT_ready")
        s_ks = sem("k_scaled")
        s_sc = sem("ret_scores")
        s_p = sem("ret_probs")
        s_ro = sem("ret_out_psum")
        s_roe = sem("ret_out_ready")
        s_rsc = sem("ret_s_scores")
        s_rp = sem("ret_s_probs")
        s_rso = sem("ret_s_out")
        s_rsoe = sem("ret_s_out_ready")
        s_vs = sem("v_by_seq_ready")
        s_rkv = sem("ret_kv")
        s_rkve = sem("ret_kv_added")
        s_rst = sem("ret_state_psum")
        s_rste = sem("ret_state_ready")
        s_gat = sem("gaT_psum")
        s_gate = sem("gaT_ready")
        s_z = sem("gate_psum")
        s_ze = sem("gate_logits")
        s_l = sem("softplus")
        s_ls = sem("log_gates")
        s_gx = sem("decay_psum")
        s_gxe = sem("decays")
        s_gm = sem("gated_qk")
        s_gt = sem("gla_transposed")
        s_gte = sem("glaT_ready")
        s_gs = sem("gla_scores")
        s_gp = sem("gla_probs")
        s_kv = sem("gla_kv")
        s_sg = sem("gla_state")
        s_go = sem("gla_out_psum")
        s_goe = sem("gla_out_ready")
        s_qm = sem("gla_q_by_seq")
        s_gvs = sem("gla_v_by_seq")
        s_gkv = sem("gla_s_kv")
        s_gkve = sem("gla_s_kv_added")
        s_nq = sem("head_squares")
        s_nv = sem("head_vars")
        s_nr = sem("head_rstd")
        s_ng = sem("gates_silu")
        s_nd = sem("heads_done")
        s_mt = sem("mix_transposed")
        s_mte = sem("mixT_ready")
        s_wout = sem("w_out_in")
        s_wo = sem("mix_psum")
        s_q1 = sem("mix_square_sum")
        s_r1 = sem("mix_rstd")
        s_x1 = sem("x1_ready")
        s_q2 = sem("x1_square_sum")
        s_r2 = sem("x1_rstd")
        s_h2 = sem("h2_ready")
        s_h2d = [sem("h2_stored0"), sem("h2_stored1")]
        s_h2t = sem("h2_transposed")
        s_h2T = sem("h2T_ready")
        s_xr = [sem("x_again0"), sem("x_again1")]
        s_lg = sem("logits")
        s_sig = sem("router_scores")
        s_tk = sem("experts_taken")
        s_pos = sem("positions")
        s_pend = sem("block_ends")
        s_blk = sem("block_counts")
        s_rch = sem("blocks_in_reach")
        s_trow = sem("table_psum")
        s_tab = sem("table_ready")
        s_wsh = sem("w_shared_in")
        s_sgu = sem("shared_gate_up")
        s_ssi = sem("shared_silu")
        s_sm = sem("shared_act")
        s_sht = sem("shared_actT_psum")
        s_shte = sem("shared_actT")
        s_sy = sem("shared_psum")
        s_sye = sem("shared_ready")
        s_wgu = [sem(f"w_gate_up_in{b}") for b in range(U)]
        s_wdn = [sem(f"w_down_in{b}") for b in range(U)]
        s_dhi = sem("w_down_high_ready")
        s_dlo = sem("w_down_low_ready")
        s_oh = sem("onehot_ready")
        s_info = sem("slot_info_psum")
        s_kept = sem("slot_info_kept_ready")
        s_idx = sem("gather_index_ready")
        s_xg = [sem("x_rows_in0"), sem("x_rows_in1")]
        s_xt = sem("xT_psum")
        s_xta = sem("xT_low_ready")
        s_xtv = sem("xT_high_ready")
        s_gu = sem("gate_up_psum")
        s_si = sem("silu_ready")
        s_act = sem("act_ready")
        s_at = sem("actT_psum")
        s_ate = sem("actT_ready")
        s_y = sem("y_psum")
        s_ya = sem("y_low_ready")
        s_yv = sem("y_high_ready")
        s_ys = [sem(f"y_rows_out{b}") for b in range(U)]
        s_tick = sem("rows_scattered")
        s_free = sem("y_rows_free")
        s_wt = sem("slot_weight_and_row_ready")
        s_pulse = sem("gpsimd_pulse")
        s_sq = sem("head_squares_ready")
        s_rowtile = sem("row_tile_changed")
        s_hw = sem("head_weights_in")
        s_yb = [sem("y_again0"), sem("y_again1")]
        s_add = sem("combined")
        s_q3 = sem("ffn_square_sum")
        s_r3 = sem("ffn_rstd")
        s_fin = sem("out_ready")
        s_out = sem("outputs_stored")

        GS_BANK, GO_BANK = (5, 0), (7, 1)
        block = ctx.enter_context(nc.Block())

        def tok_rows(a_prompt, a_sample, t):
            return a_prompt[0, t * P:(t + 1) * P, :] if t < PT else a_sample.rearrange("b s d -> (b s) d")

        def last_turn(eng):
            return eng.value_load(tab[0:1, 3, 0:1], min_val=-(-MIN_BLOCKS // U) - 1, max_val=-(-MAX_BLOCKS // U) - 1)

        @block.sync
        def _(sp):
            sp.dma_start(cond[0:1, :], c_prompt[:, :]).then_inc(s_cond, 16)
            sp.dma_start(cond[1:NCOND, :], c_sample[:, :]).then_inc(s_cond, 16)
            sp.dma_start(arena[:, 0:CONST_W], consts).then_inc(s_const, 16)
            ada = w_ada[0].rearrange("(k p) n -> p k n", p=P)
            for b in range(2):
                sp.dma_start(w_ada_buf[:, b], ada[:, :, b * 512:(b + 1) * 512]).then_inc(s_wada[b], 16)
            sp.dma_start(ada_bias, b_ada[0:1, :].broadcast_to([NCOND, 6 * D])).then_inc(s_rows, 16)
            for n, w in enumerate((norm_pre_mix, norm_post_mix, norm_pre_ffn, norm_post_ffn)):
                sp.dma_start(norm_rows[:, n], w[0:1, :].broadcast_to([NCOND, D])).then_inc(s_rows, 16)
            with sp.Fori(1, 6) as i:
                for b in range(2):
                    sp.wait_ge(s_mod, 2 * i + b - 1)
                    sp.dma_start(w_ada_buf[:, b], ada[:, :, bass.ds((2 * i + b) * 512, 512)]).then_inc(s_wada[b], 16)
            for t in range(2):
                sp.dma_start(x_buf[0:ROWS[t], t % 2], tok_rows(x_prompt, x_sample, t)).then_inc(s_x[t % 2], 16)
            sp.dma_start(gate_up[:, :], gla_gate_up[0]).then_inc(s_small, 16)
            sp.dma_start(gate_bias[:, :], gla_gate_bias[0:1, :].broadcast_to([P, GK_W])).then_inc(s_small, 16)
            sp.dma_start(w_router_buf[:, :, :], w_router[0].rearrange("(p k) e -> p k e", k=KT)).then_inc(s_small, 16)
            sp.dma_start(r_bias[:, :], router_bias[0:1, :].broadcast_to([P, E])).then_inc(s_small, 16)
            sp.wait_ge(s_mod, 12)
            win = w_in[0].rearrange("(k p) n -> p k n", p=P)
            sp.dma_start(w_in_buf, win[:, :, 0:GW]).then_inc(s_win, 16)
            sp.wait_ge(s_fold, 4)
            for n, at in enumerate((2, 3, 4, 5)):
                sp.dma_start(mod_rows[:, n * D:(n + 1) * D], mod[0:NCOND, at * D:(at + 1) * D]).then_inc(s_mst, 16)
            for t in range(2, NT):
                sp.wait_ge(s_h, t - 1)
                sp.dma_start(x_buf[0:ROWS[t], t % 2], tok_rows(x_prompt, x_sample, t)).then_inc(s_x[t % 2], 16)
            with sp.Fori(1, NG) as g:
                sp.wait_ge(s_wlo, g)
                sp.dma_start(w_in_buf, win[:, :, bass.ds(g * GW, GW)]).then_inc(s_win, 16)
            sp.wait_ge(s_pj, NG * NT)
            sp.dma_start(s0_ret, state_ret[0].rearrange("b h d v -> d b h v")).then_inc(s_st, 16)
            for h in range(H):
                sp.dma_start(s0_gla[(h % 2) * GK:(h % 2 + 1) * GK, :, h // 2, :],
                             state_gla[0, :, h].rearrange("b d v -> d b v")).then_inc(s_st, 16)
            for n, w in enumerate((w_sh_gate, w_sh_up)):
                sp.dma_start(w_sh[:, :, n * FF:(n + 1) * FF],
                             w[0].rearrange("(p k) f -> p k f", k=KT)).then_inc(s_wsh, 16)
            sp.dma_start(w_sh_down_buf, w_sh_down[0].rearrange("(p k) d -> p k d", k=FK)).then_inc(s_wsh, 16)
            sp.wait_ge(s_rste, 1)
            sp.dma_start(ret_p[0, 0].rearrange("h d v -> d h v"), ret_out).then_inc(s_out, 16)
            sp.wait_ge(s_rkve, 2 * H)
            sp.dma_start(ret_s[0].rearrange("b h d v -> d b h v"), s0_ret).then_inc(s_out, 16)
            sp.wait_ge(s_rso, H)
            sp.wait_ge(s_ro, H)
            for n, w in enumerate((ret_norm_w, ret_norm_b, gla_norm_w)):
                sp.dma_start(head_w[:, n], w.rearrange("a h v -> a (h v)").broadcast_to([P, RET_W])).then_inc(s_hw, 16)
            sp.wait_ge(s_sg, NCH)
            for h in range(H):
                sp.dma_start(gla_p[0, 0, h], s_gla[(h % 2) * GK:(h % 2 + 1) * GK, NCH, h // 2, :]).then_inc(s_out, 16)
            sp.wait_ge(s_gkve, 2 * H)
            for h in range(H):
                sp.dma_start(gla_s[0, :, h].rearrange("b d v -> d b v"),
                             s0_gla[(h % 2) * GK:(h % 2 + 1) * GK, :, h // 2, :]).then_inc(s_out, 16)
            sp.wait_ge(s_goe, NT)
            sp.wait_ge(s_out, 16 * (2 + 2 * H))
            sp.dma_start(w_out_buf, w_out[0].rearrange("(k p) n -> p k n", p=P)).then_inc(s_wout, 16)
            sp.dma_start(bc2[:, 0:3].rearrange("p c d -> p (c d)"), mod_rows[0:1, 0:3 * D].broadcast_to([P, 3 * D])).then_inc(s_bc2, 16)
            for b in range(SB):
                sp.dma_start(bc2[b * SS:(b + 1) * SS, 3:6].rearrange("p c d -> p (c d)"),
                             mod_rows[1 + b:2 + b, 0:3 * D].broadcast_to([SS, 3 * D])).then_inc(s_bc2, 16)
            for t in range(NT):
                if t >= 2:
                    sp.wait_ge(s_x1, t - 1)
                sp.dma_start(x_buf[0:ROWS[t], t % 2], tok_rows(x_prompt, x_sample, t)).then_inc(s_xr[t % 2], 16)
                if t == 2:
                    sp.dma_start(bcg2[:, 0], mod_rows[0:1, 3 * D:4 * D].broadcast_to([P, D])).then_inc(s_bcg, 16)
                    for b in range(SB):
                        sp.dma_start(bcg2[b * SS:(b + 1) * SS, 1],
                                     mod_rows[1 + b:2 + b, 3 * D:4 * D].broadcast_to([SS, D])).then_inc(s_bcg, 16)
            for t in range(NT):
                sp.wait_ge(s_h2, t + 1)
                sp.dma_start(h2_rows[t * P:t * P + ROWS[t], :], h2_buf[0:ROWS[t], t % 2]).then_inc(s_h2d[t % 2], 16)

            def load_block(j, b, wait):
                r = b % RING
                e = sp.value_load(tab[0:1, 2, bass.ds(j, 1)] if not isinstance(j, int) else tab[0:1, 2, j:j + 1],
                                  min_val=0, max_val=E - 1)
                if wait:
                    sp.wait_ge(s_gu, j - RING + 1)
                gate = w_exp_gate[0, bass.ds(e, 1)].rearrange("a (p k) f -> (a p) k f", k=KT)
                up = w_exp_up[0, bass.ds(e, 1)].rearrange("a (p k) f -> (a p) k f", k=KT)
                down = w_exp_down[0, bass.ds(e, 1)].rearrange("a (p k) d -> (a p) k d", k=FK)
                sp.dma_start(w_gu[r][:, 0], gate).then_inc(s_wgu[b], 16)
                sp.dma_start(w_gu[r][:, 1], up).then_inc(s_wgu[b], 16)
                if wait:
                    sp.wait_ge(s_dlo, j - RING + 1)
                sp.dma_start(w_dn[r], down).then_inc(s_wdn[b], 16)

            sp.wait_ge(s_tab, 1)
            sp.wait_ge(s_wo, NT)
            sp.wait_ge(s_h2, NT)
            for j in range(U):
                load_block(j, j, j >= RING)
            last = last_turn(sp)
            with sp.Fori(0, last) as i:
                for b in range(U):
                    load_block(i * U + (U + b), b, True)
            sp.wait_ge(s_y, last * U + U)
            sp.wait_ge(s_tick, 1)
            rows_by_tok = expert_rows.rearrange("(n k) d -> n k d", k=TOPK)
            for t in range(NT):
                if t >= 2:
                    sp.wait_ge(s_add, t - 1)
                sp.dma_start(y_buf[t % 2][0:ROWS[t]], rows_by_tok[t * P:t * P + ROWS[t]]).then_inc(s_yb[t % 2], 16)
                if t >= 1:
                    sp.wait_ge(s_fin, t)
                    sp.dma_start(tok_rows(y_prompt, y_sample, t - 1), out_buf[0:ROWS[t - 1], (t - 1) % 2]).then_inc(s_out, 16)
            sp.wait_ge(s_fin, NT)
            sp.dma_start(tok_rows(y_prompt, y_sample, NT - 1), out_buf[0:ROWS[NT - 1], (NT - 1) % 2]).then_inc(s_out, 16)
            sp.wait_ge(s_out, 16 * (2 + 2 * H + NT))

        @block.gpsimd
        def _(g):
            steps = [0]

            def step(ins):
                steps[0] += 1
                ins.then_inc(s_g, 1)
                g.wait_ge(s_g, steps[0])

            g.sem_inc(s_free, 2)
            step(g.memset(minus_half[:, :], -0.5))

            def inverse_root(out, total, cols, width, ready):
                step(g.tensor_scalar(out, total, 1.0 / width, EPS, ALU.mult, ALU.add))
                g.tensor_tensor(out, out, minus_half[0:out.shape[0], 0:cols], ALU.pow).then_inc(ready, 1)

            for t in range(NT):
                R = ROWS[t]
                g.wait_ge(s_ss, t + 1)
                inverse_root(rstd[0:R, 0, t:t + 1], ss[0:R, 0, t:t + 1], 1, D, s_rs)
            for t in range(NT):
                R = ROWS[t]
                g.wait_ge(s_nv, t + 1)
                inverse_root(head_rs[0:R, t], head_ss[0:R, t], 2 * H, DV, s_nr)
            for t in range(NT):
                R = ROWS[t]
                g.wait_ge(s_q1, t + 1)
                inverse_root(rstd[0:R, 1, t:t + 1], ss[0:R, 1, t:t + 1], 1, D, s_r1)
                g.wait_ge(s_q2, t + 1)
                inverse_root(rstd[0:R, 2, t:t + 1], ss[0:R, 2, t:t + 1], 1, D, s_r2)

            last_gather = g.to_reg(N - 1)
            last_scatter = g.to_reg(N * TOPK - 1)

            def gather(j, b, wait=True):
                g.wait_ge(s_idx, j + 1)
                if wait:
                    g.wait_ge(s_xt, j - 1)
                g.sem_inc(s_pulse, 1)
                g.indirect_dma_start(x_rows[0:T, b % 2], None, h2_rows[:, :],
                                     bass.IndirectOffsetOnAxis(token_idx[0:T, b:b + 1].bitcast(U32), 0),
                                     bounds_check=last_gather, oob_is_err=False).then_inc(s_xg[b % 2], 16)

            def scatter(j, b):
                g.wait_ge(s_ya, j + 2)
                g.wait_ge(s_yv, j + 2)
                g.sem_inc(s_pulse, 1)
                g.indirect_dma_start(expert_rows[:, :], bass.IndirectOffsetOnAxis(row_idx[0:T, b:b + 1].bitcast(U32), 0),
                                     y_rows[0:T, b % 2], None, bounds_check=last_scatter,
                                     oob_is_err=False).then_inc(s_ys[b], 16)

            g.wait_ge(s_sye, NT)
            step(g.memset(x_rows, 0.0))
            g.wait_ge(s_h2, NT)
            g.wait_ge(s_h2d[0], 48)
            g.wait_ge(s_h2d[1], 32)
            g.wait_ge(s_tab, 1)
            for j in range(GATHER_AHEAD):
                gather(j, j, j >= 2)

            def turn(i, is_last):
                for b in range(U):
                    if not is_last or b + GATHER_AHEAD < U:
                        gather(i * U + (b + GATHER_AHEAD), (b + GATHER_AHEAD) % U)
                    scatter(i * U + b, b)
                    g.wait_ge(s_ys[b], 16 * i + 16)
                    g.sem_inc(s_free, 1)

            last = last_turn(g)
            with g.Fori(0, last) as i:
                turn(i, False)
            turn(last, True)
            g.sem_inc(s_tick, 1)
            for t in range(NT):
                R = ROWS[t]
                g.wait_ge(s_q3, t + 1)
                inverse_root(rstd[0:R, 3, t:t + 1], ss[0:R, 3, t:t + 1], 1, D, s_r3)

        @block.scalar
        def _(a):
            steps = [0]

            def step(ins):
                steps[0] += 1
                ins.then_inc(s_a, 1)
                a.wait_ge(s_a, steps[0])

            def high_part(g, b):
                a.wait_ge(s_win, 16 * g + 16)
                if not (isinstance(g, int) and g < 2):
                    a.wait_ge(s_pj, g * NT - NT)
                a.activation(w_hi[b][:, :, :], w_in_buf, ACT.Copy).then_inc(s_whi, 1)

            a.sem_inc(s_pj_ev, NT)
            a.sem_inc(s_ya, 1)
            a.wait_ge(s_cond, 32)
            a.activation(cond, cond, ACT.Silu).then_inc(s_silu, 1)
            for n in range(4):
                a.wait_ge(s_bc, n + 1)
                R = P if n < 2 else NS
                a.activation(bc1[0:R, n].rearrange("p (c n) -> p c n", c=2), ps[0:R, 2 * n:2 * n + 2], ACT.Copy).then_inc(s_bc_ev, 1)
            for t in range(NT):
                R = ROWS[t]
                a.wait_ge(s_x[t % 2], 16 * (t // 2 + 1))
                if t:
                    a.wait_ge(s_ss, t)
                a.activation(square_junk[0:R], x_buf[0:R, t % 2], ACT.Square, accum_out=ss[0:R, 0, t:t + 1]).then_inc(s_ss, 1)
                if t == 0:
                    a.wait_ge(s_mst, 64)
                for half in range(2):
                    a.wait_ge(s_tr, 2 * t + half + 1)
                    a.activation(hT_hi[:, 4 * half:4 * half + 4, t * P:t * P + R],
                                 ps[:, (2 * t + half) % 4].rearrange("p (k r) -> p k r", k=4)[:, :, 0:R],
                                 ACT.Copy).then_inc(s_hT, 1)
                if t == 1:
                    high_part(0, 0)

            def projected(g):
                for t in range(NT):
                    a.wait_ge(s_pj, g * NT + (t + 1))
                    a.activation(proj[0:ROWS[t], t, bass.ds(g * GW, GW)], ps[0:ROWS[t], t, 0:GW],
                                 ACT.Copy).then_inc(s_pj_ev, 1)

            a.wait_ge(s_h, NT)
            high_part(1, 1)
            projected(0)
            with a.Fori(1, NG // 2) as i:
                for b in range(2):
                    high_part(i * 2 + b, b)
                    projected(i * 2 + (b - 1))
            projected(NG - 1)
            for t in range(NT):
                R = ROWS[t]
                for half in range(2):
                    a.wait_ge(s_rtr, 2 * t + half + 1)
                    a.activation(qkT[:, 4 * half:4 * half + 4, t * P:t * P + R],
                                 ps[:, (2 * t + half) % 4].rearrange("p (k r) -> p k r", k=4)[:, :, 0:R],
                                 ACT.Copy).then_inc(s_qkT, 1)
            for h in range(H):
                a.wait_ge(s_ro, h + 1)
                a.activation(proj[:, 0:PT, C_RQ + h * DV:C_RQ + (h + 1) * DV],
                             ps[:, 6 + h % 2].rearrange("p (t v) -> p t v", t=PT), ACT.Copy).then_inc(s_roe, 1)
                a.wait_ge(s_rso, h + 1)
                a.activation(proj[0:NS, PT, C_RQ + h * DV:C_RQ + (h + 1) * DV], ps[0:NS, 2, 0:DV],
                             ACT.Copy).then_inc(s_rsoe, 1)
            a.wait_ge(s_rst, 1)
            a.activation(ret_out, ps[:, 0].rearrange("p (h v) -> p h v", h=H), ACT.Copy).then_inc(s_rste, 1)
            a.wait_ge(s_ze, NT)
            parts = ((softplus[:, 0:PT], z_buf[:, 0:PT]), (softplus[0:NS, PT], z_buf[0:NS, PT]))
            for to, z in parts:
                step(a.activation(to, z, ACT.Abs))
            for to, z in parts:
                step(a.activation(to, to, ACT.Exp, scale=-1.0))
            for to, z in parts:
                a.activation(to, to, ACT.Ln, bias=1.0).then_inc(s_l, 1)
            for t in range(NT):
                R = ROWS[t]
                a.wait_ge(s_gx, t + 1)
                if t >= 2:
                    a.wait_ge(s_gm, t - 1)
                e, d, end = ex[0:R, t % 2], ps[0:R, 2 * (t % 2)], ps[:, 2 * (t % 2) + 1]
                a.activation(e[:, 0], d[:, 0:GK_W], ACT.Exp).then_inc(s_gxe, 1)
                a.activation(e[:, 1], d[:, 0:GK_W], ACT.Exp, scale=-1.0).then_inc(s_gxe, 1)
                a.activation(e[:, 2], d[:, GK_W:2 * GK_W], ACT.Exp).then_inc(s_gxe, 1)
                a.activation(e[:, 3], end[0:R, 0:GK_W], ACT.Exp).then_inc(s_gxe, 1)
                nc_, to = (2, dec[:, :, 2 * t:2 * t + 2]) if t < PT else (SB, dec_s)
                a.activation(to, end[:, GK_W:GK_W + nc_ * HP].rearrange("p (h c) -> p h c", h=HP), ACT.Exp).then_inc(s_gxe, 1)
            for t in range(NT):
                R = ROWS[t]
                for n in range(2):
                    a.wait_ge(s_gt, 2 * t + n + 1)
                    if n == 0 and t:
                        a.wait_ge(s_go, t)
                    a.activation(glT[:, :, n, 0:R], ps[:, 3 + n].rearrange("p (k r) -> p k r", k=4)[:, 0:3, 0:R],
                                 ACT.Copy).then_inc(s_gte, 1)
                a.wait_ge(s_go, t + 1)
                for odd in range(2):
                    o = a.activation(proj[0:R, t, C_GO:C_GO + RET_W].rearrange("p (h v) -> p h v", h=H)[:, odd:H:2],
                                     ps[0:R, GO_BANK[odd]].rearrange("p (h v) -> p h v", h=H)[:, odd:H:2], ACT.Copy)
                    if odd:
                        o.then_inc(s_goe, 1)
                    else:
                        step(o)
            for t in range(NT):
                R = ROWS[t]
                step(a.activation(proj[0:R, t, C_RG:C_RG + RET_W], proj[0:R, t, C_RG:C_RG + RET_W], ACT.Silu))
                a.activation(proj[0:R, t, C_GG:C_GG + RET_W], proj[0:R, t, C_GG:C_GG + RET_W], ACT.Silu).then_inc(s_ng, 1)
            for t in range(NT):
                R = ROWS[t]
                a.wait_ge(s_nq, t + 1)
                step(a.activation(proj[0:R, t, C_RK:C_RK + RET_W], proj[0:R, t, C_RQ:C_RQ + RET_W], ACT.Square))
                a.activation(proj[0:R, t, C_RV:C_RV + RET_W], proj[0:R, t, C_GO:C_GO + RET_W], ACT.Square).then_inc(s_sq, 1)
            for t in range(NT):
                R = ROWS[t]
                for half in range(2):
                    a.wait_ge(s_mt, 2 * t + half + 1)
                    a.activation(hT[:, 4 * half:4 * half + 4, t * P:t * P + R],
                                 ps[:, 4 + half].rearrange("p (k r) -> p k r", k=4)[:, :, 0:R],
                                 ACT.Copy).then_inc(s_mte, 1)
            for t in range(NT):
                R = ROWS[t]
                a.wait_ge(s_wo, t + 1)
                a.activation(sq_junk2[0:R].rearrange("p (c n) -> p c n", c=2), ps[0:R, 2 * (t % 2):2 * (t % 2) + 2],
                             ACT.Square, accum_out=ss[0:R, 1, t:t + 1]).then_inc(s_q1, 1)
                a.wait_ge(s_q1, t + 1)
                a.wait_ge(s_x1, t + 1)
                a.activation(sq_junk2[0:R], x1[0:R, t], ACT.Square, accum_out=ss[0:R, 2, t:t + 1]).then_inc(s_q2, 1)
                a.wait_ge(s_q2, t + 1)
                for half in range(2):
                    a.wait_ge(s_h2t, 2 * t + half + 1)
                    a.activation(hT[:, 4 * half:4 * half + 4, t * P:t * P + R],
                                 ps[:, 6 + half].rearrange("p (k r) -> p k r", k=4)[:, :, 0:R],
                                 ACT.Copy).then_inc(s_h2T, 1)
            for t in range(NT):
                R = ROWS[t]
                a.wait_ge(s_lg, t + 1)
                a.activation(scores[0:R, t], ps[0:R, 6 + t % 2, 0:E], ACT.Sigmoid).then_inc(s_sig, 1)
            for t in range(NT):
                R = ROWS[t]
                a.wait_ge(s_sgu, t + 1)
                if t >= 2:
                    a.wait_ge(s_sm, t - 1)
                a.activation(sh_silu[0:R, t % 2], ps[0:R, t % 2, 0:FF], ACT.Silu).then_inc(s_ssi, 1)
            for t in range(NT):
                R = ROWS[t]
                a.wait_ge(s_sht, t + 1)
                a.activation(sh_actT[:, t, :, 0:R], ps[:, 2 + t % 2, 0:FK * P].rearrange("p (k r) -> p k r", k=FK)[:, :, 0:R],
                             ACT.Copy).then_inc(s_shte, 1)
            for t in range(NT):
                R = ROWS[t]
                a.wait_ge(s_sy, t + 1)
                a.activation(shared[0:R, t].rearrange("p (c n) -> p c n", c=2), ps[0:R, 4 + 2 * (t % 2):6 + 2 * (t % 2)],
                             ACT.Copy).then_inc(s_sye, 1)

            def silu(j, b):
                a.wait_ge(s_gu, j + 1)
                a.activation(silu_g[0:T, b % 2], ps[0:T, b % 2, 0:FF], ACT.Silu).then_inc(s_si, 1)

            def x_low(j, b):
                a.wait_ge(s_xt, j + 1)
                a.activation(xT[:, b % 2, 0:4, :], ps[:, 4, 0:4 * T].rearrange("p (k r) -> p k r", k=4), ACT.Copy).then_inc(s_xta, 1)

            def down_high(j, b, turns):
                a.wait_ge(s_wdn[b % U], 16 * turns)
                if not (isinstance(j, int) and j < 1):
                    a.wait_ge(s_y, j)
                a.activation(down_hi[:, :, :], w_dn[b % RING], ACT.Copy).then_inc(s_dhi, 1)

            a.wait_ge(s_tab, 1)
            a.wait_ge(s_sye, NT)
            for j in range(2):
                x_low(j, j)
                if j == 0:
                    silu(0, 0)
                    down_high(0, 0, 1)

            def turn(i, is_last):
                for b in range(U):
                    if not is_last or b + 1 < U:
                        silu(i * U + (b + 1), b + 1)
                    if not is_last or b + 2 < U:
                        x_low(i * U + (b + 2), b + 2)
                    a.wait_ge(s_y, i * U + (b + 1))
                    a.wait_ge(s_wt, i * (2 * U) + (2 * b + 2))
                    a.wait_ge(s_free, i * U + (b + 1))
                    a.activation(y_rows[0:T, b % 2, 0:512], ps[0:T, 2], ACT.Copy, scale=slot_w[0:T, b:b + 1]).then_inc(s_ya, 1)
                    if not is_last or b + 1 < U:
                        down_high(i * U + (b + 1), b + 1, i + ((b + 1) // U + 1))

            last = last_turn(a)
            with a.Fori(0, last) as i:
                turn(i, False)
            turn(last, True)
            for t in range(NT):
                R = ROWS[t]
                a.wait_ge(s_add, t + 1)
                a.activation(sq2[0:R], y_buf[t % 2][0:R, 0], ACT.Square, accum_out=ss[0:R, 3, t:t + 1]).then_inc(s_q3, 1)
                a.wait_ge(s_q3, t + 1)

        @block.vector
        def _(v):
            steps = [0]

            def step(ins):
                steps[0] += 1
                ins.then_inc(s_v, 1)
                v.wait_ge(s_v, steps[0])

            def mark(ins, s, k):
                ins.then_inc(s, 1)
                v.wait_ge(s, k)

            def hT_low_part(t):
                R = ROWS[t]
                for half in range(2):
                    v.wait_ge(s_hT, 2 * t + half + 1)
                    at = (slice(None), slice(4 * half, 4 * half + 4), slice(t * P, t * P + R))
                    v.tensor_tensor(hT_lo[at], ps[:, (2 * t + half) % 4].rearrange("p (k r) -> p k r", k=4)[:, :, 0:R],
                                    hT_hi[at].bitcast(F32), ALU.subtract).then_inc(s_hTl, 1)

            def low_part(g, b):
                v.wait_ge(s_whi, g + 1)
                v.tensor_tensor(w_lo[b][:, :, :], w_in_buf, w_hi[b][:, :, :].bitcast(F32), ALU.subtract).then_inc(s_wlo, 1)

            v.sem_inc(s_mod_ev, 2)
            v.sem_inc(s_yv, 1)
            v.wait_ge(s_cT, 1)
            v.tensor_copy(condT[:, :, :], ps[:, 0, 0:KT * NCOND].rearrange("p (k c) -> p k c", k=KT)).then_inc(s_cTs, 1)
            v.wait_ge(s_rows, 16 * 5)
            with v.Fori(0, 6) as i:
                for b in range(2):
                    v.wait_ge(s_mod, 2 * i + b + 1)
                    v.tensor_tensor(mod[0:NCOND, bass.ds((2 * i + b) * 512, 512)], ps[0:NCOND, b],
                                    ada_bias[:, bass.ds((2 * i + b) * 512, 512)], ALU.add).then_inc(s_mod_ev, 1)
            v.wait_ge(s_mod_ev, 2 + 12)
            for at, n, one in ((1, 0, 1.0), (2, 1, 0.0), (4, 2, 1.0), (5, 3, 0.0)):
                m = mod[0:NCOND, at * D:(at + 1) * D]
                mark(v.scalar_tensor_tensor(out=m, in0=m, scalar=one, in1=norm_rows[:, n], op0=ALU.add, op1=ALU.mult),
                     s_fold, {1: 1, 2: 2, 4: 3, 5: 4}[at])
            for t in range(NT):
                R = ROWS[t]
                if t == 0:
                    v.wait_ge(s_bc_ev, 4)
                A, S = (0, 1) if t < PT else (2, 3)
                v.wait_ge(s_x[t % 2], 16 * (t // 2 + 1))
                v.wait_ge(s_rs, t + 1)
                if t >= 2:
                    v.wait_ge(s_tr, 2 * (t - 1))
                step(v.scalar_tensor_tensor(out=h_buf[0:R, t % 2], in0=x_buf[0:R, t % 2], scalar=rstd[0:R, 0, t:t + 1],
                                            in1=bc1[0:R, A], op0=ALU.mult, op1=ALU.mult))
                mark(v.tensor_tensor(h_buf[0:R, t % 2], h_buf[0:R, t % 2], bc1[0:R, S], ALU.add), s_h, t + 1)
                if t == 0:
                    v.wait_ge(s_mst, 64)
                else:
                    hT_low_part(t - 1)
                if t == 2:
                    low_part(0, 0)
            hT_low_part(PT)

            def rotate(t):
                R = ROWS[t]
                qk = proj[0:R, t, 0:2 * RET_W].rearrange("p (h c d) -> p h c d", h=2 * H, c=2)
                lo, hi = qk[:, :, 0], qk[:, :, 1]
                c = K("cos", R)[:, t * 64:(t + 1) * 64].unsqueeze(1).broadcast_to([R, 2 * H, 64])
                s = K("sin", R)[:, t * 64:(t + 1) * 64].unsqueeze(1).broadcast_to([R, 2 * H, 64])
                r4 = [rot[0:R, n].rearrange("p (h d) -> p h d", h=2 * H) for n in range(4)]
                for n, (x, f) in enumerate(((lo, c), (hi, s), (lo, s), (hi, c))):
                    step(v.tensor_tensor(r4[n], x, f, ALU.mult))
                step(v.tensor_tensor(lo, r4[0], r4[1], ALU.subtract))
                mark(v.tensor_tensor(hi, r4[2], r4[3], ALU.add), s_rot, t + 1)

            low_part(1, 1)
            with v.Fori(1, 3) as i:
                for b in range(2):
                    low_part(i * 2 + b, b)
            for g in range(6, NG):
                low_part(g, g % 2)
                if g - 6 < NT:
                    v.wait_ge(s_pj_ev, (1 + (2 * RET_W - 1) // GW + 1) * NT)
                    rotate(g - 6)
            v.wait_ge(s_pj_ev, (NG + 1) * NT)
            v.wait_ge(s_small, 16 * 4)
            for t in range(NT):
                R = ROWS[t]
                v.wait_ge(s_rtr, 2 * t + 2)
                kk = proj[0:R, t, C_RK:C_RK + RET_W].rearrange("p (h d) -> p h d", h=H)
                kp = K("kpow", R)[:, t * H:(t + 1) * H].unsqueeze(2).broadcast_to([R, H, DK])
                mark(v.tensor_tensor(kk, kk, kp, ALU.mult), s_ks, t + 1)
            v.wait_ge(s_st, 16 * (1 + H))
            for h in range(H):
                for J in range(PT):
                    n = SEQ - J * P
                    v.wait_ge(s_sc, PT * h + J + 1)
                    if J == 0 and h >= 2:
                        v.wait_ge(s_ro, h - 1)
                    mark(v.tensor_tensor(pr[:, h % 2, PR_OFF[J]:PR_OFF[J] + n], ps[:, 4 + J % 2, 0:n],
                                         K("dret")[:, h * SEQ:h * SEQ + n], ALU.mult), s_p, PT * h + J + 1)
                v.wait_ge(s_rsc, h + 1)
                if h:
                    v.wait_ge(s_rso, h)
                    v.wait_ge(s_rkv, 2 * h)
                step(v.tensor_tensor(qg_r, qkT[:, h, SEQ:N], K("qpow_s")[:, h * NS:(h + 1) * NS], ALU.mult))
                step(v.tensor_tensor(qm_r, qg_r.unsqueeze(1).broadcast_to([P, SB, NS]),
                                     K("seq_cols").rearrange("p (b n) -> p b n", b=SB), ALU.mult))
                mark(v.tensor_tensor(pr_s, ps[0:NS, 1, 0:NS], K("dret_s", NS)[:, h * NS:(h + 1) * NS], ALU.mult), s_rp, h + 1)
                mark(v.tensor_tensor(v_by_seq,
                                     proj[0:NS, PT, C_RV + h * DV:C_RV + (h + 1) * DV].unsqueeze(1).broadcast_to([NS, SB, DV]),
                                     K("seq_rows", NS).unsqueeze(2).broadcast_to([NS, SB, DV]), ALU.mult), s_vs, h + 1)
                v.wait_ge(s_rso, h + 1)
                for half in range(2):
                    v.wait_ge(s_rkv, 2 * h + half + 1)
                    st = s0_ret[:, half * 4:half * 4 + 4, h, :]
                    mark(v.scalar_tensor_tensor(out=st, in0=st, scalar=float(np.float32(GAMMA[h] ** SS)),
                                                in1=ps[:, 3].rearrange("p (b v) -> p b v", b=4),
                                                op0=ALU.mult, op1=ALU.add), s_rkve, 2 * h + half + 1)
            v.wait_ge(s_rste, 1)
            v.wait_ge(s_out, 32)
            for n in range(NT + 1):
                if n < NT:
                    v.wait_ge(s_gat, n + 1)
                    if n >= 2:
                        v.wait_ge(s_z, n - 1)
                    mark(v.tensor_copy(gaT[n % 2][:, 0:ROWS[n]], ps[0:RANK, n % 2, 0:ROWS[n]]), s_gate, n + 1)
                if n:
                    t = n - 1
                    v.wait_ge(s_z, t + 1)
                    v.tensor_tensor(z_buf[0:ROWS[t], t], ps[0:ROWS[t], 2 + t % 2, 0:GK_W], gate_bias[0:ROWS[t], :],
                                    ALU.add).then_inc(s_ze, 1)
            v.wait_ge(s_roe, H)
            v.wait_ge(s_rsoe, H)
            for t in range(NT):
                R = ROWS[t]
                o = proj[0:R, t, C_RQ:C_RQ + RET_W].rearrange("p (h v) -> p h v", h=H)
                step(v.tensor_reduce(head_mu[0:R], o, AX.X, ALU.add))
                step(v.tensor_scalar(head_mu[0:R], head_mu[0:R], 1.0 / DV, None, ALU.mult))
                mark(v.tensor_tensor(o, o, head_mu[0:R].unsqueeze(2).broadcast_to([R, H, DV]), ALU.subtract), s_nq, t + 1)
            v.wait_ge(s_l, 2)
            for part in ((slice(0, P), slice(0, PT)), (slice(0, NS), PT)):
                v.scalar_tensor_tensor(out=ls_buf[part], in0=z_buf[part], scalar=0.0, in1=softplus[part],
                                       op0=ALU.min, op1=ALU.subtract).then_inc(s_ls, 1)
            for t in range(NT):
                R = ROWS[t]
                v.wait_ge(s_gxe, 5 * (t + 1))
                q, k = proj[0:R, t, C_GQ:C_GQ + GK_W], proj[0:R, t, C_GK:C_GK + GK_W]
                sc = GK ** -0.5
                step(v.scalar_tensor_tensor(out=gated[0:R, t, 0], in0=q, scalar=sc, in1=ex[0:R, t % 2, 2], op0=ALU.mult, op1=ALU.mult))
                step(v.tensor_tensor(gated[0:R, t, 1], k, ex[0:R, t % 2, 3], ALU.mult))
                step(v.scalar_tensor_tensor(out=q, in0=q, scalar=sc, in1=ex[0:R, t % 2, 0], op0=ALU.mult, op1=ALU.mult))
                mark(v.tensor_tensor(k, k, ex[0:R, t % 2, 1], ALU.mult), s_gm, t + 1)
            step(v.memset(s_gla[:, 0], 0.0))
            for t in range(NT):
                R = ROWS[t]
                v.wait_ge(s_gs, t + 1)
                m = K("maskg", P) if t < PT else K("maskg_s", NS)
                for odd in range(2):
                    o = v.tensor_tensor(p_gla[0:R, odd:H:2, 0:R],
                                        ps[0:R, GS_BANK[odd]].rearrange("p (h r) -> p h r", h=H)[:, odd:H:2, 0:R],
                                        m.unsqueeze(1).broadcast_to([R, HP, R]), ALU.mult)
                    if odd:
                        mark(o, s_gp, t + 1)
                    else:
                        step(o)
                if t < PT:
                    for c in range(2):
                        n = 2 * t + c
                        v.wait_ge(s_kv, n + 1)
                        for hh in range(2):
                            rows = slice(hh * GK, (hh + 1) * GK)
                            for hp in range(HP):
                                o = v.scalar_tensor_tensor(
                                    out=s_gla[rows, n + 1, hp], in0=s_gla[rows, n, hp], scalar=dec[rows, hp, n:n + 1],
                                    in1=ps[rows, 6, (2 * hp + hh) * DV:(2 * hp + hh + 1) * DV], op0=ALU.mult, op1=ALU.add)
                                if hh == 1 and hp == HP - 1:
                                    mark(o, s_sg, n + 1)
                                else:
                                    step(o)
                else:
                    v.wait_ge(s_gte, 2 * NT)
                    for hp in range(HP):
                        mark(v.tensor_tensor(qm_g[:, hp], glT[:, 2, hp, 0:NS].unsqueeze(1).broadcast_to([P, SB, NS]),
                                             K("seq_cols").rearrange("p (b n) -> p b n", b=SB), ALU.mult), s_qm, hp + 1)
                    for h in range(H):
                        rows, hp = slice((h % 2) * GK, (h % 2 + 1) * GK), h // 2
                        if h:
                            v.wait_ge(s_gkv, 2 * h)
                        mark(v.tensor_tensor(v_by_seq_g,
                                             proj[0:NS, PT, C_GV + h * DV:C_GV + (h + 1) * DV].unsqueeze(1).broadcast_to([NS, SB, DV]),
                                             K("seq_rows", NS).unsqueeze(2).broadcast_to([NS, SB, DV]), ALU.mult), s_gvs, h + 1)
                        v.wait_ge(s_go, NT)
                        for half in range(2):
                            st = s0_gla[rows, half * 4:half * 4 + 4, hp, :]
                            step(v.tensor_tensor(st, st, dec_s[rows, hp, half * 4:half * 4 + 4].unsqueeze(2).broadcast_to([GK, 4, DV]), ALU.mult))
                            v.wait_ge(s_gkv, 2 * h + half + 1)
                            mark(v.tensor_tensor(st, st, ps[rows, 6].rearrange("p (b v) -> p b v", b=4), ALU.add),
                                 s_gkve, 2 * h + half + 1)
            v.wait_ge(s_goe, NT)
            v.wait_ge(s_hw, 48)
            for t in range(NT):
                R = ROWS[t]
                v.wait_ge(s_sq, t + 1)
                mark(v.tensor_reduce(head_ss[0:R, t], proj[0:R, t, C_RK:C_RK + 2 * RET_W].rearrange("p (h v) -> p h v", h=2 * H), AX.X, ALU.add), s_nv, t + 1)
            for t in range(NT):
                R = ROWS[t]
                v.wait_ge(s_nr, t + 1)
                v.wait_ge(s_ng, t + 1)
                for n, (at, gate) in enumerate(((C_RQ, C_RG), (C_GO, C_GG))):
                    o = proj[0:R, t, at:at + RET_W]
                    o3 = o.rearrange("p (h v) -> p h v", h=H)
                    step(v.tensor_tensor(o3, o3, head_rs[0:R, t, n * H:(n + 1) * H].unsqueeze(2).broadcast_to([R, H, DV]), ALU.mult))
                    step(v.tensor_tensor(o, o, head_w[0:R, 2 * n], ALU.mult))
                    if n == 0:
                        step(v.tensor_tensor(o, o, head_w[0:R, 1], ALU.add))
                        step(v.tensor_tensor(o, o, proj[0:R, t, gate:gate + RET_W], ALU.mult))
                    else:
                        mark(v.tensor_tensor(o, o, proj[0:R, t, gate:gate + RET_W], ALU.mult), s_nd, t + 1)
            v.wait_ge(s_mt, 2 * NT)
            step(v.memset(taken[:, PT, :], 0.0))
            step(v.memset(info_tab, 0.0))
            step(v.memset(zeros[:, :], 0.0))
            step(v.memset(gsc[:, 0:TOPG], 1.0e30))
            v.wait_ge(s_bc2, 16 * (1 + SB))
            for t in range(NT):
                R = ROWS[t]
                o = 0 if t < PT else 3
                v.wait_ge(s_r1, t + 1)
                v.wait_ge(s_xr[t % 2], 16 * (t // 2 + 1))
                step(v.scalar_tensor_tensor(out=x1[0:R, t].rearrange("p (c n) -> p c n", c=2),
                                            in0=ps[0:R, 2 * (t % 2):2 * (t % 2) + 2], scalar=rstd[0:R, 1, t:t + 1],
                                            in1=bc2[0:R, o].rearrange("p (c n) -> p c n", c=2), op0=ALU.mult, op1=ALU.mult))
                mark(v.tensor_tensor(x1[0:R, t], x1[0:R, t], x_buf[0:R, t % 2], ALU.add), s_x1, t + 1)
                v.wait_ge(s_r2, t + 1)
                if t >= 2:
                    v.wait_ge(s_h2t, 2 * (t - 1))
                    v.wait_ge(s_h2d[t % 2], 16 * (t // 2))
                tmp = bc2_tmp[0:R]
                step(v.scalar_tensor_tensor(out=tmp, in0=x1[0:R, t], scalar=rstd[0:R, 2, t:t + 1], in1=bc2[0:R, o + 2],
                                            op0=ALU.mult, op1=ALU.mult))
                mark(v.tensor_tensor(h2_buf[0:R, t % 2].rearrange("q (k p) -> q k p", k=KT),
                                     tmp.rearrange("q (p k) -> q k p", k=KT),
                                     bc2[0:R, o + 1].rearrange("q (p k) -> q k p", k=KT), ALU.add), s_h2, t + 1)
            for t in range(NT):
                R = ROWS[t]
                v.wait_ge(s_sig, t + 1)
                sc, se = scores[0:R, t], sel[0:R]
                step(v.tensor_tensor(se, sc, r_bias[0:R], ALU.add))
                for n in range(G):
                    step(v.max(out=top8[0:R, n], in_=se[:, n * 8:(n + 1) * 8]))
                step(v.tensor_tensor(gsc[0:R, TOPG:], top8[0:R, :, 0], top8[0:R, :, 1], ALU.add))
                step(v.max(out=m8[0:R], in_=gsc[0:R]))
                step(v.match_replace(out=gsc2[0:R], in_to_replace=m8[0:R], in_values=gsc[0:R], imm_value=-1.0e30))
                step(v.tensor_tensor(gsc2[0:R, TOPG:], gsc2[0:R, TOPG:], gsc[0:R, TOPG:], ALU.not_equal))
                gm = gsc2[0:R, TOPG:].unsqueeze(2).broadcast_to([R, G, E // G])
                se3 = se.rearrange("p (g n) -> p g n", g=G)
                step(v.tensor_tensor(se3, se3, gm, ALU.mult))
                step(v.tensor_scalar(gsc2[0:R, TOPG:], gsc2[0:R, TOPG:], 1.0e30, -1.0e30, ALU.mult, ALU.add))
                step(v.tensor_tensor(se3, se3, gm, ALU.add))
                step(v.max(out=m8[0:R], in_=se))
                step(v.match_replace(out=sel2[0:R], in_to_replace=m8[0:R], in_values=se, imm_value=-3.0e38))
                tk = taken[0:R, t]
                step(v.tensor_tensor(tk, sel2[0:R], se, ALU.not_equal))
                step(v.tensor_tensor(sel2[0:R], sc, tk, ALU.mult))
                step(v.tensor_reduce(wsum[0:R, 0:1], sel2[0:R], AX.X, ALU.add))
                step(v.reciprocal(wsum[0:R, 1:2], wsum[0:R, 0:1]))
                inf = info_tab[0:R].rearrange("p (e t c) -> p e t c", e=ECOL, t=NT)[:, 0:E, t]
                step(v.tensor_scalar(inf[:, :, 2], sel2[0:R], wsum[0:R, 1:2], SCALE, ALU.mult, ALU.mult))
                step(v.tensor_scalar(inf[:, :, 0], tk, 0.0, K("tok", R)[:, t:t + 1], ALU.mult, ALU.add))
                step(v.tensor_tensor_scan(sel2[0:R], tk, zeros[0:R], 0.0, ALU.add, ALU.add))
                mark(v.tensor_scalar(inf[:, :, 1], sel2[0:R], K("tok8", R)[:, t:t + 1], None, ALU.add), s_tk, t + 1)
                v.wait_ge(s_ssi, t + 1)
                mark(v.tensor_tensor(sh_act[0:R, t].rearrange("q (k p) -> q k p", k=FK),
                                     sh_silu[0:R, t % 2].rearrange("q (p k) -> q k p", k=FK),
                                     ps[0:R, t % 2, FF:2 * FF].rearrange("q (p k) -> q k p", k=FK), ALU.mult), s_sm, t + 1)
            v.wait_ge(s_pos, 1)
            pt = pos_tab.rearrange("p (c e t) -> p c e t", c=MAXC, e=ECOL)
            step(v.memset(pos_tab, -FAR))
            step(v.tensor_scalar(taken_far[:, :, :], taken[:, :, :], FAR, -FAR, ALU.mult, ALU.add))
            step(v.tensor_tensor(pt[:, 0, 0:E, :].rearrange("p e t -> p t e"), taken_far[:, :, :],
                                 ps[:, 0, 0:NT * E].rearrange("p (t e) -> p t e", t=NT), ALU.add))
            for c in range(1, MAXC):
                step(v.tensor_scalar(pt[:, c, 0:E, :], pt[:, 0, 0:E, :], -float(c * T), None, ALU.add))
            cnt, nb = blocks_e[:, 0:1], blocks_e[:, 1:2]
            step(v.tensor_copy(cnt, ps[0:E, 1, 0:1]))
            step(v.tensor_scalar(nb, cnt, 0.0, None, ALU.is_gt))
            for c in range(1, MAXC):
                o = v.scalar_tensor_tensor(out=nb, in0=cnt, scalar=float(c * T), in1=nb, op0=ALU.is_gt, op1=ALU.add)
                if c < MAXC - 1:
                    step(o)
                else:
                    mark(o, s_blk, 1)
            v.wait_ge(s_pend, 1)
            step(v.tensor_copy(blocks_e[:, 2:3], ps[0:E, 2, 0:1]))
            mark(v.tensor_scalar(in_reach[:, :], K("count", E), blocks_e[:, 2:3], None, ALU.is_ge), s_rch, 1)
            v.wait_ge(s_trow, 1)
            e_row, c_row, n_row = rowf[:, 0], rowf[:, 1], rowf[:, 2]
            step(v.tensor_copy(e_row, ps[0:1, 3, 0:P]))
            step(v.tensor_tensor(c_row, K("count", 1), ps[0:1, 3, P:2 * P], ALU.subtract))
            step(v.tensor_scalar(c_row, c_row, float(MAXC - 1), None, ALU.min))
            step(v.scalar_tensor_tensor(out=c_row, in0=c_row, scalar=float(ECOL), in1=e_row, op0=ALU.mult, op1=ALU.add))
            step(v.tensor_scalar(tab[:, 0], c_row, float(NT), None, ALU.mult))
            step(v.tensor_scalar(tab[:, 1], e_row, float(NT * 3), None, ALU.mult))
            step(v.tensor_scalar(tab[:, 2], e_row, float(E - 1), None, ALU.min))
            step(v.tensor_copy(rowf[:, 3, 0:1], ps[0:1, 3, 2 * P:2 * P + 1]))
            step(v.tensor_scalar(n_row, K("count", 1), float(U), rowf[:, 3, 0:1], ALU.mult, ALU.is_lt))
            step(v.tensor_reduce(rowf[:, 4, 0:1], n_row, AX.X, ALU.add))
            step(v.tensor_scalar(rowf[:, 4, 0:1], rowf[:, 4, 0:1], -1.0, None, ALU.add))
            mark(v.tensor_copy(tab[:, 3, 0:1], rowf[:, 4, 0:1]), s_tab, 1)
            def slots(j, b):
                col = v.value_load(tab[0:1, 0, bass.ds(j, 1)] if not isinstance(j, int) else tab[0:1, 0, j:j + 1],
                                   min_val=0, max_val=(MAXC * ECOL - 1) * NT)
                e = v.value_load(tab[0:1, 1, bass.ds(j, 1)] if not isinstance(j, int) else tab[0:1, 1, j:j + 1],
                                 min_val=0, max_val=E * NT * 3)
                v.tensor_copy(info[:, b % 2], info_tab[:, bass.ds(e, NT * 3)]).then_inc(s_oh, 1)
                v.tensor_tensor(onehot[:, b % 2], K("count")[:, 0:T].unsqueeze(1).broadcast_to([P, NT, T]),
                                pos_tab[:, bass.ds(col, NT)].unsqueeze(2).broadcast_to([P, NT, T]),
                                ALU.is_equal).then_inc(s_oh, 1)

            def slot_info(j, b):
                v.wait_ge(s_info, j + 1)
                at = 3 * j if isinstance(j, int) else j * 3
                v.tensor_copy(slot_info_kept[0:T, bass.ds(at, 3)], ps[0:T, 7, 0:3]).then_inc(s_kept, 1)
                v.tensor_scalar(token_idx[0:T, b:b + 1], ps[0:T, 7, 0:1], EMPTY, None, ALU.add).then_inc(s_idx, 1)

            def row_and_weight(j, b):
                v.wait_ge(s_kept, j + 1)
                at = 3 * j if isinstance(j, int) else j * 3
                v.tensor_copy(slot_w[0:T, b:b + 1], slot_info_kept[0:T, bass.ds(at + 2, 1)]).then_inc(s_wt, 1)
                v.tensor_scalar(row_idx[0:T, b:b + 1], slot_info_kept[0:T, bass.ds(at + 1, 1)], EMPTY, None,
                                ALU.add).then_inc(s_wt, 1)

            def act(j, b):
                v.wait_ge(s_si, j + 1)
                v.tensor_tensor(act_rows[0:T, b % 2].rearrange("q (k p) -> q k p", k=FK),
                                silu_g[0:T, b % 2].rearrange("q (p k) -> q k p", k=FK),
                                ps[0:T, b % 2, FF:2 * FF].rearrange("q (p k) -> q k p", k=FK), ALU.mult).then_inc(s_act, 1)

            def act_T(j, b):
                v.wait_ge(s_at, j + 1)
                raw = ps[:, 6, 0:FK * T].rearrange("p (k r) -> p k r", k=FK)
                v.tensor_copy(actT_hi[:, b % 2], raw).then_inc(s_ate, 1)
                v.wait_ge(s_ate, j * 2 + 1)
                v.tensor_tensor(actT_lo[:, b % 2], raw, actT_hi[:, b % 2].bitcast(F32), ALU.subtract).then_inc(s_ate, 1)

            def down_low(j, b):
                v.wait_ge(s_dhi, j + 1)
                v.tensor_tensor(down_lo[:, :, :], w_dn[b % RING], down_hi[:, :, :].bitcast(F32), ALU.subtract).then_inc(s_dlo, 1)

            def x_high(j, b):
                v.wait_ge(s_xt, j + 1)
                v.tensor_copy(xT[:, b % 2, 4:8, :], ps[:, 5, 0:4 * T].rearrange("p (k r) -> p k r", k=4)).then_inc(s_xtv, 1)

            v.wait_ge(s_sye, NT)
            v.wait_ge(s_h2d[0], 48)
            v.wait_ge(s_h2d[1], 32)
            for j in range(AHEAD):
                slots(j, j)
                slot_info(j, j)
            row_and_weight(0, 0)
            x_high(0, 0)
            act(0, 0)
            act_T(0, 0)
            down_low(0, 0)
            x_high(1, 1)

            def turn(i, is_last):
                for b in range(U):
                    if not is_last or b + 1 < U:
                        act(i * U + (b + 1), b + 1)
                    if not is_last or b + 2 < U:
                        x_high(i * U + (b + 2), b + 2)
                    if not is_last or b + AHEAD < U:
                        slots(i * U + (b + AHEAD), b + AHEAD)
                    v.wait_ge(s_y, i * U + (b + 1))
                    v.wait_ge(s_wt, i * (2 * U) + (2 * b + 2))
                    v.wait_ge(s_free, i * U + (b + 1))
                    v.tensor_scalar(y_rows[0:T, b % 2, 512:1024], ps[0:T, 3], slot_w[0:T, b:b + 1], None, ALU.mult).then_inc(s_yv, 1)
                    if not is_last or b + 1 < U:
                        act_T(i * U + (b + 1), b + 1)
                        row_and_weight(i * U + (b + 1), (b + 1) % U)
                        down_low(i * U + (b + 1), b + 1)
                    if not is_last or b + AHEAD < U:
                        slot_info(i * U + (b + AHEAD), (b + AHEAD) % U)

            last = last_turn(v)
            with v.Fori(0, last) as i:
                turn(i, False)
            turn(last, True)
            v.wait_ge(s_bcg, 16 * (1 + SB))
            for t in range(NT):
                R = ROWS[t]
                o = t // PT
                v.wait_ge(s_yb[t % 2], 16 * (t // 2 + 1))
                y = y_buf[t % 2][0:R]
                step(v.tensor_tensor(y[:, 0:4], y[:, 0:4], y[:, 4:8], ALU.add))
                step(v.tensor_tensor(y[:, 0:2], y[:, 0:2], y[:, 2:4], ALU.add))
                step(v.tensor_tensor(y[:, 0], y[:, 0], y[:, 1], ALU.add))
                mark(v.tensor_tensor(y[:, 0], y[:, 0], shared[0:R, t], ALU.add), s_add, t + 1)
                v.wait_ge(s_r3, t + 1)
                if t >= 2:
                    v.wait_ge(s_out, 16 * (2 + 2 * H + t - 1))
                ob = out_buf[0:R, t % 2]
                step(v.scalar_tensor_tensor(out=ob, in0=y[:, 0], scalar=rstd[0:R, 3, t:t + 1], in1=bcg2[0:R, o],
                                            op0=ALU.mult, op1=ALU.mult))
                mark(v.tensor_tensor(ob, ob, x1[0:R, t], ALU.add), s_fin, t + 1)

        @block.tensor
        def _(pe):
            pe.wait_ge(s_const, 16)
            pe.wait_ge(s_silu, 1)
            for k in range(KT):
                o = pe.transpose(ps[:, 0, k * NCOND:(k + 1) * NCOND], cond[:, k * P:(k + 1) * P], ident[0:NCOND, 0:NCOND])
            o.then_inc(s_cT, 1)
            pe.wait_ge(s_cTs, 1)
            with pe.Fori(0, 6) as i:
                for b in range(2):
                    pe.wait_ge(s_wada[b], 16 * i + 16)
                    pe.wait_ge(s_mod_ev, 2 * i + b + 1)
                    for k in range(KT):
                        o = pe.matmul(ps[0:NCOND, b], condT[:, k, :], w_ada_buf[:, b, k], start=(k == 0), stop=(k == KT - 1))
                    o.then_inc(s_mod, 1)

            pe.wait_ge(s_fold, 4)

            def broadcast(col, sample, bank):
                sel_rows = K("sels", NCOND) if sample else K("selp", NCOND)
                R = NS if sample else P
                for half in range(2):
                    o = pe.matmul(ps[0:R, bank + half], sel_rows, mod[0:NCOND, col * D + half * 512:col * D + half * 512 + 512],
                                  start=True, stop=True)
                o.then_inc(s_bc, 1)

            for n, (col, sample) in enumerate(((1, 0), (0, 0), (1, 1), (0, 1))):
                broadcast(col, sample, 2 * n)
            pe.wait_ge(s_bc_ev, 4)

            def transpose_rows(src, t, banks, done, free, ahead, base=0):
                R = ROWS[t]
                for half in range(2):
                    n = 2 * t + half
                    if n >= ahead:
                        pe.wait_ge(free, base + n - ahead + 1)
                    for k in range(4):
                        kk = 4 * half + k
                        o = pe.transpose(ps[:, banks + n % ahead, k * P:k * P + R], src(kk), ident[0:R, 0:R])
                    o.then_inc(done, 1)

            for t in range(NT):
                pe.wait_ge(s_h, t + 1)
                transpose_rows(lambda k: h_buf[0:ROWS[t], t % 2, k * P:(k + 1) * P], t, 0, s_tr, s_hTl, 4)
            pe.wait_ge(s_hTl, 2 * NT)
            with pe.Fori(0, NG // 2) as i:
                for b in range(2):
                    pe.wait_ge(s_wlo, 2 * i + b + 1)
                    for t in range(NT):
                        pe.wait_ge(s_pj_ev, (2 * i + b) * NT + t + 1)
                        cols = slice(t * P, t * P + ROWS[t])
                        for k in range(KT):
                            for n, (x, w) in enumerate(((hT_hi, w_hi[b]), (hT_hi, w_lo[b]), (hT_lo, w_hi[b]))):
                                o = pe.matmul(ps[0:ROWS[t], t, 0:GW], x[:, k, cols], w[:, k],
                                              start=(k == 0 and n == 0), stop=(k == KT - 1 and n == 2))
                        o.then_inc(s_pj, 1)
            pe.wait_ge(s_pj_ev, (NG + 1) * NT)
            for t in range(NT):
                pe.wait_ge(s_rot, t + 1)
                transpose_rows(lambda k: proj[0:ROWS[t], t, k * P:(k + 1) * P], t, 0, s_rtr, s_qkT, 4)
            pe.wait_ge(s_qkT, 2 * NT)
            pe.wait_ge(s_ks, NT)
            pe.wait_ge(s_st, 16 * (1 + H))
            for h in range(H):
                for J in range(PT):
                    n = SEQ - J * P
                    if PT * h + J >= 2:
                        pe.wait_ge(s_p, PT * h + J - 1)
                    pe.matmul(ps[:, 4 + J % 2, 0:n], qkT[:, H + h, J * P:(J + 1) * P], qkT[:, h, J * P:SEQ],
                              start=True, stop=True).then_inc(s_sc, 1)
                if h:
                    pe.wait_ge(s_rp, h)
                pe.matmul(ps[0:NS, 1, 0:NS], qkT[:, H + h, SEQ:N], qkT[:, h, SEQ:N], start=True, stop=True).then_inc(s_rsc, 1)
                for J in range(PT):
                    o = pe.matmul(ps[:, 0, h * DV:(h + 1) * DV], proj[:, J, C_RK + h * DK:C_RK + (h + 1) * DK],
                                  proj[:, J, C_RV + h * DV:C_RV + (h + 1) * DV], start=(J == 0), stop=(J == PT - 1))
                if h == H - 1:
                    o.then_inc(s_rst, 1)
                pe.wait_ge(s_p, PT * (h + 1))
                if h >= 2:
                    pe.wait_ge(s_roe, h - 1)
                for I in range(PT):
                    for J in range(I + 1):
                        at = PR_OFF[J] + (I - J) * P
                        o = pe.matmul(ps[:, 6 + h % 2, I * DV:(I + 1) * DV], pr[:, h % 2, at:at + P],
                                      proj[:, J, C_RV + h * DV:C_RV + (h + 1) * DV], start=(J == 0), stop=(J == I))
                o.then_inc(s_ro, 1)
                pe.wait_ge(s_rp, h + 1)
                if h:
                    pe.wait_ge(s_rsoe, h)
                pe.matmul(ps[0:NS, 2, 0:DV], pr_s, proj[0:NS, PT, C_RV + h * DV:C_RV + (h + 1) * DV], start=True, stop=False)
                for b in range(SB):
                    o = pe.matmul(ps[0:NS, 2, 0:DV], qm_r[:, b], s0_ret[:, b, h], start=False, stop=(b == SB - 1))
                o.then_inc(s_rso, 1)
                pe.wait_ge(s_vs, h + 1)
                for half in range(2):
                    if 2 * h + half:
                        pe.wait_ge(s_rkve, 2 * h + half)
                    pe.matmul(ps[:, 3], proj[0:NS, PT, C_RK + h * DK:C_RK + (h + 1) * DK],
                              v_by_seq[:, half * 4:half * 4 + 4].rearrange("p b v -> p (b v)"), start=True, stop=True).then_inc(s_rkv, 1)
            pe.wait_ge(s_rste, 1)
            pe.wait_ge(s_rsoe, H)
            pe.wait_ge(s_rkve, 2 * H)
            for n in range(NT + 1):
                if n < NT:
                    if n >= 2:
                        pe.wait_ge(s_gate, n - 1)
                    R = ROWS[n]
                    pe.transpose(ps[0:RANK, n % 2, 0:R], proj[0:R, n, C_GA:C_GA + RANK], ident[0:R, 0:R]).then_inc(s_gat, 1)
                if n:
                    t = n - 1
                    pe.wait_ge(s_gate, t + 1)
                    if t >= 2:
                        pe.wait_ge(s_ze, t - 1)
                    pe.matmul(ps[0:ROWS[t], 2 + t % 2, 0:GK_W], gaT[t % 2][:, 0:ROWS[t]], gate_up[:, :],
                              start=True, stop=True).then_inc(s_z, 1)
            pe.wait_ge(s_ls, 2)
            for t in range(NT):
                R = ROWS[t]
                sfx = "" if t < PT else "_s"
                if t >= 2:
                    pe.wait_ge(s_gxe, 5 * (t - 1))
                d, end, ls = ps[0:R, 2 * (t % 2)], ps[:, 2 * (t % 2) + 1], ls_buf[0:R, t]
                pe.matmul(d[:, 0:GK_W], K("gmid" + sfx, R), ls, start=True, stop=True)
                pe.matmul(d[:, GK_W:2 * GK_W], K("gcum" + sfx, R), ls, start=True, stop=True)
                pe.matmul(end[0:R, 0:GK_W], K("gend" + sfx, R), ls, start=True, stop=True)
                nc_ = 2 if t < PT else SB
                for hp in range(HP):
                    o = pe.matmul(end[:, GK_W + hp * nc_:GK_W + (hp + 1) * nc_], ls[:, hp * P:(hp + 1) * P],
                                  K("chunk" + sfx, R), start=True, stop=True)
                o.then_inc(s_gx, 1)
            for t in range(NT):
                R = ROWS[t]
                pe.wait_ge(s_gm, t + 1)
                if t == 0:
                    pe.wait_ge(s_gxe, 5 * NT)
                for n in range(2):
                    if t:
                        pe.wait_ge(s_gte, 2 * (t - 1) + n + 1)
                    for w, src in enumerate((proj[0:R, t, C_GQ:C_GQ + GK_W], proj[0:R, t, C_GK:C_GK + GK_W], gated[0:R, t, 0])):
                        o = pe.transpose(ps[:, 3 + n, w * P:w * P + R], src[:, n * P:(n + 1) * P], ident[0:R, 0:R])
                    o.then_inc(s_gt, 1)
                pe.wait_ge(s_gte, 2 * t + 2)
                if t:
                    pe.wait_ge(s_gp, t)
                for h in range(H):
                    rows, hp = slice((h % 2) * GK, (h % 2 + 1) * GK), h // 2
                    o = pe.matmul(ps[0:R, GS_BANK[h % 2], h * P:h * P + R], glT[rows, 1, hp, 0:R], glT[rows, 0, hp, 0:R], start=True, stop=True)
                o.then_inc(s_gs, 1)
                if t < PT:
                    for c in range(2):
                        n = 2 * t + c
                        if n:
                            pe.wait_ge(s_sg, n)
                        crow = slice(c * CH, (c + 1) * CH)
                        for hp in range(HP):
                            o = pe.matmul(ps[:, 6, 2 * hp * DV:2 * (hp + 1) * DV], gated[crow, t, 1, hp * P:(hp + 1) * P],
                                          proj[crow, t, C_GV + 2 * hp * DV:C_GV + 2 * (hp + 1) * DV], start=True, stop=True)
                        o.then_inc(s_kv, 1)
                pe.wait_ge(s_gp, t + 1)
                if t:
                    pe.wait_ge(s_goe, t)
                if t < PT:
                    pe.wait_ge(s_sg, 2 * t + 1)
                else:
                    pe.wait_ge(s_qm, HP)
                for h in range(H):
                    rows, hp = slice((h % 2) * GK, (h % 2 + 1) * GK), h // 2
                    out = ps[0:R, GO_BANK[h % 2], h * DV:(h + 1) * DV]
                    o = pe.matmul(out, p_gla[0:R, h, 0:R], proj[0:R, t, C_GV + h * DV:C_GV + (h + 1) * DV], start=True, stop=False)
                    if t == PT and h % 2:
                        o.then_inc(s_rowtile, 1)
                        pe.wait_ge(s_rowtile, h)
                    if t < PT:
                        for c in range(2):
                            o = pe.matmul(ps[c * CH:(c + 1) * CH, GO_BANK[h % 2], h * DV:(h + 1) * DV], glT[rows, 2, hp, c * CH:(c + 1) * CH],
                                          s_gla[rows, 2 * t + c, hp], start=False, stop=True)
                    else:
                        for b in range(SB):
                            o = pe.matmul(out, qm_g[rows, hp, b], s0_gla[rows, b, hp], start=False, stop=(b == SB - 1))
                        if h == 1:
                            o.then_inc(s_rowtile, 1)
                            pe.wait_ge(s_rowtile, 2)
                o.then_inc(s_go, 1)
            for h in range(H):
                hp = h // 2
                pe.wait_ge(s_gvs, h + 1)
                for half in range(2):
                    if 2 * h + half:
                        pe.wait_ge(s_gkve, 2 * h + half)
                    pe.matmul(ps[:, 6], gated[0:NS, PT, 1, hp * P:(hp + 1) * P],
                              v_by_seq_g[:, half * 4:half * 4 + 4].rearrange("p b v -> p (b v)"), start=True, stop=True).then_inc(s_gkv, 1)
            pe.wait_ge(s_goe, NT)
            pe.wait_ge(s_gkve, 2 * H)
            def mixed_transposed(t):
                pe.wait_ge(s_nd, t + 1)
                transpose_rows(lambda k: proj[0:ROWS[t], t, (C_RQ + k * P) if k < 4 else (C_GO + (k - 4) * P):
                                              (C_RQ + k * P + P) if k < 4 else (C_GO + (k - 4) * P + P)],
                               t, 4, s_mt, s_mte, 2)

            def out_mm(t):
                pe.wait_ge(s_mte, 2 * t + 2)
                if t >= 2:
                    pe.wait_ge(s_x1, t - 1)
                for half in range(2):
                    for k in range(KT):
                        o = pe.matmul(ps[0:ROWS[t], 2 * (t % 2) + half], hT[:, k, t * P:t * P + ROWS[t]],
                                      w_out_buf[:, k, half * 512:half * 512 + 512], start=(k == 0), stop=(k == KT - 1))
                o.then_inc(s_wo, 1)

            def h2_transposed(t):
                pe.wait_ge(s_h2, t + 1)
                transpose_rows(lambda k: h2_buf[0:ROWS[t], t % 2, k * P:(k + 1) * P], t, 6, s_h2t, s_h2T, 2)

            mixed_transposed(0)
            mixed_transposed(1)
            pe.wait_ge(s_wout, 16)
            for t in range(NT):
                if t == 2:
                    mixed_transposed(4)
                out_mm(t)
                if t < 2:
                    mixed_transposed(t + 2)
                else:
                    h2_transposed(t - 2)
            h2_transposed(NT - 2)
            h2_transposed(NT - 1)
            pe.wait_ge(s_h2T, 2 * NT)
            for t in range(NT):
                if t >= 2:
                    pe.wait_ge(s_sig, t - 1)
                for k in range(KT):
                    o = pe.matmul(ps[0:ROWS[t], 6 + t % 2, 0:E], hT[:, k, t * P:t * P + ROWS[t]], w_router_buf[:, k, :],
                                  start=(k == 0), stop=(k == KT - 1))
                o.then_inc(s_lg, 1)
            pe.wait_ge(s_wsh, 48)
            for t in range(NT):
                if t >= 2:
                    pe.wait_ge(s_sm, t - 1)
                for k in range(KT):
                    o = pe.matmul(ps[0:ROWS[t], t % 2], hT[:, k, t * P:t * P + ROWS[t]], w_sh[:, k], start=(k == 0), stop=(k == KT - 1))
                o.then_inc(s_sgu, 1)
            pe.wait_ge(s_tk, NT)
            pe.wait_ge(s_sm, NT)
            for t in range(NT):
                for u in range(t):
                    pe.matmul(ps[:, 0, t * E:(t + 1) * E], K("ones"), taken[:, u], start=(u == 0), stop=False)
                pe.matmul(ps[:, 0, t * E:(t + 1) * E], K("before"), taken[:, t], start=(t == 0), stop=True)
            for t in range(NT):
                o = pe.matmul(ps[0:E, 1, 0:1], taken[:, t], K("ones")[:, 0:1], start=(t == 0), stop=(t == NT - 1))
            o.then_inc(s_pos, 1)
            for t in range(NT):
                R = ROWS[t]
                if t >= 2:
                    pe.wait_ge(s_shte, t - 1)
                for k in range(FK):
                    o = pe.transpose(ps[:, 2 + t % 2, k * P:k * P + R], sh_act[0:R, t, k * P:(k + 1) * P], ident[0:R, 0:R])
                o.then_inc(s_sht, 1)
            pe.wait_ge(s_sig, NT)

            def shared_down(t):
                R = ROWS[t]
                if t >= 2:
                    pe.wait_ge(s_sye, t - 1)
                for half in range(2):
                    for k in range(FK):
                        o = pe.matmul(ps[0:R, 4 + 2 * (t % 2) + half], sh_actT[:, t, k, 0:R],
                                      w_sh_down_buf[:, k, half * 512:half * 512 + 512], start=(k == 0), stop=(k == FK - 1))
                o.then_inc(s_sy, 1)

            pe.wait_ge(s_shte, NT)
            shared_down(0)
            pe.wait_ge(s_blk, 1)
            pe.matmul(ps[0:E, 2, 0:1], K("upto", E), blocks_e[:, 1:2], start=True, stop=True).then_inc(s_pend, 1)
            shared_down(1)
            pe.wait_ge(s_rch, 1)
            pe.matmul(ps[0:1, 3, 0:P], K("ones", E)[:, 0:1], in_reach, start=True, stop=True)
            pe.matmul(ps[0:1, 3, P:2 * P], blocks_e[:, 1:2], in_reach, start=True, stop=True)
            pe.matmul(ps[0:1, 3, 2 * P:2 * P + 1], blocks_e[:, 1:2], K("ones", E)[:, 0:1], start=True, stop=True).then_inc(s_trow, 1)
            for t in range(2, NT):
                shared_down(t)

            def slot_info(j, b):
                pe.wait_ge(s_oh, j * 2 + 2)
                if not (isinstance(j, int) and j < 1):
                    pe.wait_ge(s_idx, j)
                    pe.wait_ge(s_kept, j)
                for t in range(NT):
                    o = pe.matmul(ps[0:T, 7, 0:3], onehot[:, b % 2, t], info[:, b % 2, t * 3:(t + 1) * 3],
                                  start=(t == 0), stop=(t == NT - 1))
                o.then_inc(s_info, 1)

            def x_transposed(i, b):
                pe.wait_ge(s_xg[b % 2], 16 * (i * (U // 2) + (b // 2 + 1)))
                for k in range(KT):
                    o = pe.transpose(ps[:, 4 + k // 4, (k % 4) * T:(k % 4 + 1) * T], x_rows[0:T, b % 2, k * P:(k + 1) * P],
                                     ident[0:T, 0:T])
                o.then_inc(s_xt, 1)

            def gate_up_mm(j, b, turns):
                pe.wait_ge(s_wgu[b % U], 32 * turns)
                pe.wait_ge(s_xta, j + 1)
                pe.wait_ge(s_xtv, j + 1)
                for k in range(KT):
                    o = pe.matmul(ps[0:T, b % 2], xT[:, b % 2, k], w_gu[b % RING][:, :, k, :], start=(k == 0), stop=(k == KT - 1))
                o.then_inc(s_gu, 1)

            def act_transposed(j, b):
                pe.wait_ge(s_act, j + 1)
                for k in range(FK):
                    o = pe.transpose(ps[:, 6, k * T:(k + 1) * T], act_rows[0:T, b % 2, k * P:(k + 1) * P], ident[0:T, 0:T])
                o.then_inc(s_at, 1)

            def down_mm(j, b):
                pe.wait_ge(s_dlo, j + 1)
                pe.wait_ge(s_ate, j * 2 + 2)
                pe.wait_ge(s_ya, j + 1)
                pe.wait_ge(s_yv, j + 1)
                for half in range(2):
                    for k in range(FK):
                        for n, (x, w) in enumerate(((actT_hi, down_hi), (actT_hi, down_lo), (actT_lo, down_hi))):
                            o = pe.matmul(ps[0:T, 2 + half], x[:, b % 2, k], w[:, k, half * 512:half * 512 + 512],
                                          start=(k == 0 and n == 0), stop=(k == FK - 1 and n == 2))
                o.then_inc(s_y, 1)

            pe.wait_ge(s_sye, NT)
            for j in range(AHEAD):
                slot_info(j, j)
            x_transposed(0, 0)
            gate_up_mm(0, 0, 1)
            act_transposed(0, 0)
            x_transposed(0, 1)

            def turn(i, is_last):
                for b in range(U):
                    if not is_last or b + 1 < U:
                        gate_up_mm(i * U + (b + 1), b + 1, i + ((b + 1) // U + 1))
                    if not is_last or b + 2 < U:
                        x_transposed(i, b + 2)
                    down_mm(i * U + b, b)
                    if not is_last or b + 1 < U:
                        act_transposed(i * U + (b + 1), b + 1)
                    if not is_last or b + AHEAD < U:
                        slot_info(i * U + (b + AHEAD), b + AHEAD)

            last = last_turn(pe)
            with pe.Fori(0, last) as i:
                turn(i, False)
            turn(last, True)


def kernel(**inputs):
    import concourse.bacc as bacc
    from concourse.bass_utils import run_bass_kernel_spmd

    nc = bacc.Bacc("TRN2", target_bir_lowering=False, num_devices=1)
    names = ["x_prompt", "x_sample", "state_ret", "state_gla", "c_prompt", "c_sample", "w_ada", "b_ada", "norm_pre_mix",
             "norm_post_mix", "norm_pre_ffn", "norm_post_ffn", "w_in", "gla_gate_up", "gla_gate_bias", "ret_norm_w",
             "ret_norm_b", "gla_norm_w", "w_out", "w_router", "router_bias", "w_exp_gate", "w_exp_up", "w_exp_down",
             "w_sh_gate", "w_sh_up", "w_sh_down"]
    arrays, args = {}, []
    for name in names:
        arrays["in_" + name] = np.ascontiguousarray(inputs[name])
    arrays["in_consts"] = _constants()
    for name in names + ["consts"]:
        a = arrays["in_" + name]
        args.append(nc.dram_tensor("in_" + name, a.shape, mybir.dt.from_np(a.dtype), kind="ExternalInput").ap())
    outs = [("y_prompt", (1, SEQ, D)), ("y_sample", (SB, SS, D)), ("ret_prompt", (1, 1, H, DK, DV)),
            ("gla_prompt", (1, 1, H, GK, DV)), ("ret_sample", (1, SB, H, DK, DV)), ("gla_sample", (1, SB, H, GK, DV))]
    for name, shape in outs:
        args.append(nc.dram_tensor("out_" + name, shape, F32, kind="ExternalOutput").ap())
    args.append(nc.dram_tensor("mod_rows", (NCOND, 4 * D), F32, kind="Internal").ap())
    args.append(nc.dram_tensor("h2_rows", (N, D), F32, kind="Internal").ap())
    args.append(nc.dram_tensor("expert_rows", (N * TOPK, D), F32, kind="Internal").ap())
    hybrid_step(nc, *args)
    r = run_bass_kernel_spmd(nc, [arrays], core_ids=[0])
    return tuple(r.results[0]["out_" + name] for name, _ in outs)
```
